# Optimizing a Trainium2 kernel written in Bass

```python
import math
import jax, jax.numpy as jnp
from jax import lax
import numpy as np

D_MODEL = 2048
BATCH = 1
SEQ = 256
DEPTH = 2

CHUNK = 64

N_A = DEPTH // 2
N_B = DEPTH - N_A

CONV_WIDTH = 31

SB_HEADS = 16
SB_HEAD_DIM = D_MODEL // SB_HEADS
Q_BLOCK = 128

PEER_HEADS = 8
N_KEYS = 128
N_EXPERTS = N_KEYS * N_KEYS
PEER_TOPK = 16
D_QUERY = 256
D_QHALF = D_QUERY // 2
TOKEN_BLOCK = 128

ALPHA = (2.0 * DEPTH) ** 0.25
DEEPNORM_BETA = (8.0 * DEPTH) ** -0.25
LN_EPS = 1e-5

kernel_name = "yoco_conformer_stickbreaking_peer"

def layer_norm(x, g, b):
    xf = x.astype(jnp.float32)
    mu = jnp.mean(xf, axis=-1, keepdims=True)
    var = jnp.mean(jnp.square(xf - mu), axis=-1, keepdims=True)
    y = (xf - mu) * lax.rsqrt(var + LN_EPS)
    return (y * g + b).astype(x.dtype)

def conformer_conv(x, w_in, b_in, w_dw, b_dw, ln_g, ln_b, w_out, b_out):
    h = x @ w_in + b_in
    a, gate = jnp.split(h, 2, axis=-1)
    h = a * jax.nn.sigmoid(gate)
    h = lax.conv_general_dilated(
        h, w_dw.astype(h.dtype), window_strides=(1,), padding=[(CONV_WIDTH - 1, 0)],
        dimension_numbers=("NWC", "WIO", "NWC"), feature_group_count=D_MODEL) + b_dw
    h = layer_norm(h, ln_g, ln_b)
    h = jax.nn.swish(h)
    return h @ w_out + b_out

def split_heads(t):
    b, s, _ = t.shape
    return t.reshape(b, s, SB_HEADS, SB_HEAD_DIM).transpose(0, 2, 1, 3)

def stick_breaking_attention(q, k, v):
    seq = q.shape[2]
    scale = SB_HEAD_DIM ** -0.5
    outs = []
    for blk in range(seq // Q_BLOCK):
        t0, t1 = blk * Q_BLOCK, (blk + 1) * Q_BLOCK
        qb = q[:, :, t0:t1]
        kb = k[:, :, :t1]
        vb = v[:, :, :t1]
        z = jnp.einsum("bhtd,bhsd->bhts", qb, kb,
                       preferred_element_type=jnp.float32) * scale
        t_idx = t0 + jnp.arange(Q_BLOCK)[:, None]
        s_idx = jnp.arange(t1)[None, :]
        mask = s_idx < t_idx
        log_one_minus = jnp.where(mask, jax.nn.log_sigmoid(-z), 0.0)
        log_rest = lax.cumsum(log_one_minus, axis=3, reverse=True) - log_one_minus
        att = jnp.where(mask, jnp.exp(jax.nn.log_sigmoid(z) + log_rest), 0.0)
        outs.append(jnp.einsum("bhts,bhsd->bhtd", att.astype(vb.dtype), vb))
    return jnp.concatenate(outs, axis=2)

def peer(x, w_q, sub_keys, u_tab, v_tab):
    b, s, d = x.shape
    n_tok = b * s
    xt = x.reshape(n_tok, d)
    q = (xt @ w_q).reshape(n_tok, PEER_HEADS, 2, D_QHALF)
    sc = jnp.einsum("thcd,hckd->thck", q, sub_keys,
                    preferred_element_type=jnp.float32)
    top_s, top_i = lax.top_k(sc, PEER_TOPK)
    cand_s = (top_s[:, :, 0, :, None] + top_s[:, :, 1, None, :]).reshape(
        n_tok, PEER_HEADS, PEER_TOPK * PEER_TOPK)
    cand_e = (top_i[:, :, 0, :, None] * N_KEYS + top_i[:, :, 1, None, :]).reshape(
        n_tok, PEER_HEADS, PEER_TOPK * PEER_TOPK)
    best_s, best_j = lax.top_k(cand_s, PEER_TOPK)
    experts = jnp.take_along_axis(cand_e, best_j, axis=-1)
    gates = jax.nn.softmax(best_s, axis=-1).astype(x.dtype)

    n_blk = n_tok // TOKEN_BLOCK

    def block_fn(args):
        xb, eb, gb = args
        u = u_tab[eb]
        h = jnp.einsum("thkd,td->thk", u, xb)
        coef = gb * jax.nn.gelu(h, approximate=False)
        return jnp.einsum("thk,thkd->td", coef, v_tab[eb])

    out = lax.map(block_fn, (xt.reshape(n_blk, TOKEN_BLOCK, d),
                             experts.reshape(n_blk, TOKEN_BLOCK, PEER_HEADS, PEER_TOPK),
                             gates.reshape(n_blk, TOKEN_BLOCK, PEER_HEADS, PEER_TOPK)))
    return out.reshape(b, s, d)

def setup_inputs(seed: int = 0) -> dict:
    key = jax.random.key(seed)
    ks = jax.random.split(key, 20)
    D = D_MODEL
    f32 = jnp.float32
    nrm = lambda k, shape, scale: jax.random.normal(k, shape, f32) * scale
    return {
        "x": jax.random.normal(ks[0], (BATCH, SEQ, D), f32),
        "conv_w_in": nrm(ks[1], (N_A, D, 2 * D), D ** -0.5),
        "conv_b_in": nrm(ks[2], (N_A, 2 * D), 0.02),
        "conv_w_dw": nrm(ks[3], (N_A, CONV_WIDTH, 1, D), CONV_WIDTH ** -0.5),
        "conv_b_dw": nrm(ks[4], (N_A, D), 0.02),
        "conv_ln_g": 1.0 + nrm(ks[5], (N_A, D), 0.02),
        "conv_ln_b": nrm(ks[6], (N_A, D), 0.02),
        "conv_w_out": nrm(ks[7], (N_A, D, D), D ** -0.5 * DEEPNORM_BETA),
        "conv_b_out": nrm(ks[8], (N_A, D), 0.02),
        "attn_w_kv": jnp.concatenate([
            nrm(ks[9], (D, D), D ** -0.5),
            nrm(ks[10], (D, D), D ** -0.5 * DEEPNORM_BETA)], axis=1),
        "attn_w_q": nrm(ks[11], (N_B, D, D), D ** -0.5),
        "attn_w_o": nrm(ks[12], (N_B, D, D), D ** -0.5 * DEEPNORM_BETA),
        "peer_w_q": nrm(ks[13], (DEPTH, D, PEER_HEADS * D_QUERY), D ** -0.5),
        "peer_sub_keys": nrm(ks[14], (DEPTH, PEER_HEADS, 2, N_KEYS, D_QHALF), D_QHALF ** -0.5),
        "peer_u": nrm(ks[15], (DEPTH, N_EXPERTS, D), D ** -0.5),
        "peer_v": nrm(ks[16], (DEPTH, N_EXPERTS, D), DEEPNORM_BETA),
        "ln_g": 1.0 + nrm(ks[17], (DEPTH, 2, D), 0.02),
        "ln_b": nrm(ks[18], (DEPTH, 2, D), 0.02),
    }

def reference(x, conv_w_in, conv_b_in, conv_w_dw, conv_b_dw, conv_ln_g, conv_ln_b,
              conv_w_out, conv_b_out, attn_w_kv, attn_w_q, attn_w_o,
              peer_w_q, peer_sub_keys, peer_u, peer_v, ln_g, ln_b):
    k_shared = None
    v_shared = None
    for i in range(DEPTH):
        if i < N_A:
            y = conformer_conv(x, conv_w_in[i], conv_b_in[i], conv_w_dw[i], conv_b_dw[i],
                               conv_ln_g[i], conv_ln_b[i], conv_w_out[i], conv_b_out[i])
        else:
            j = i - N_A
            q = split_heads(x @ attn_w_q[j])
            o = stick_breaking_attention(q, k_shared, v_shared)
            b, _, s, _ = o.shape
            y = o.transpose(0, 2, 1, 3).reshape(b, s, D_MODEL) @ attn_w_o[j]
        x = layer_norm(ALPHA * x + y, ln_g[i, 0], ln_b[i, 0])
        x = layer_norm(ALPHA * x + peer(x, peer_w_q[i], peer_sub_keys[i], peer_u[i], peer_v[i]),
                       ln_g[i, 1], ln_b[i, 1])
        if i == N_A - 1:
            kv = x @ attn_w_kv
            k_part, v_part = jnp.split(kv, 2, axis=-1)
            k_shared = split_heads(k_part)
            v_shared = split_heads(v_part)
    return x


_drawn_inputs = setup_inputs


def setup_inputs(seed=0):
    import zlib

    import numpy as np

    out = dict(_drawn_inputs(seed))
    spreads = {}
    factors = {}
    for name, (base, spread) in spreads.items():
        noise = np.random.default_rng([zlib.crc32(name.encode()), seed]).standard_normal(out[name].shape)
        drawn = base * np.exp(spread * noise) if base else spread * noise
        out[name] = __import__('jax').numpy.asarray(drawn.astype(out[name].dtype))
    for name, factor in factors.items():
        out[name] = (out[name] * factor).astype(out[name].dtype)
    return out
```

```python
from contextlib import ExitStack

import concourse.bass as bass
from concourse import mybir

F32 = mybir.dt.float32
U32 = mybir.dt.uint32
ALU = mybir.AluOpType
ACT = mybir.ActivationFunctionType
AX_X = mybir.AxisListType.X

P = 128
LN_EPS = 1e-5
TOPK = 16
RING = 4
LN_STEPS = 10
ROUTE_LOGITS = 122
ROUTE_INDEX = 135
ROUTE_STEPS = 138


def build(nc, x, conv_w_in, conv_b_in, conv_w_dw, conv_b_dw, conv_ln_g, conv_ln_b, conv_w_out, conv_b_out,
          attn_w_kv, attn_w_q, attn_w_o, peer_w_q, peer_sub_keys, peer_u, peer_v, ln_g, ln_b, out):
    _, S, D = x.shape
    KC = D // P
    TB = S // P
    W = conv_w_dw.shape[1]
    PAD = W - 1
    HEADS = D // P
    LAYERS, PH, _, NKEY, DQ = peer_sub_keys.shape
    HC = PH * 2
    NEXP = peer_u.shape[1]
    SLOTS = PH * TOPK
    GROUPS = SLOTS // RING
    ALPHA = (2.0 * LAYERS) ** 0.25
    SCALE = float(P) ** -0.5
    Q = D // 512
    PANELS = 8
    assert TB == 2 and KC == 16 and Q == 4 and NKEY == P and DQ == P and HC == KC

    P_OUT, P_WQ = 2 * PANELS, [3 * PANELS, 8 * PANELS]
    P_K, P_V, P_Q, P_O = 4 * PANELS, 5 * PANELS, 6 * PANELS, 7 * PANELS

    with ExitStack() as ctx:
        def sb(name, shape, dt=F32):
            return ctx.enter_context(nc.sbuf_tensor(name, shape, dt))

        def sem(name):
            return ctx.enter_context(nc.semaphore(name))

        ps = ctx.enter_context(nc.psum_tensor("ps", [P, 8, 512], F32))
        x_tok = sb("x_tok", [P, TB, D])
        x_chan = sb("x_chan", [P, KC, S])
        ring = sb("ring", [P, RING, 2 * D])
        ln_rows = sb("ln_rows", [P, 2, D])
        ident = sb("ident", [P, P])
        alpha_ident = sb("alpha_ident", [P, P])
        ones = sb("ones", [P, P])
        mean_ones = sb("mean_ones", [P, P])
        tri = sb("tri", [P, P])
        causal = sb("causal", [P, P])
        iota_i = sb("iota_i", [P, TOPK], mybir.dt.int32)
        iota_f = sb("iota_f", [P, TOPK])
        NB_IN = 2 * KC
        vec = sb("vec", [P, NB_IN + 3 * KC])
        taps = sb("taps", [P, W * KC])
        stats = sb("stats", [P, TB, Q, 6])
        mv = sb("mv", [P, TB, 2])
        lnv = sb("lnv", [P, TB, 4])
        index = sb("index", [P, TB, SLOTS], U32)
        gate = sb("gate", [P, TB, SLOTS])
        index_now = sb("index_now", [P, 2, RING], U32)
        h_now = sb("h_now", [P, RING])
        gelu_now = sb("gelu_now", [P, RING])
        coef_now = sb("coef_now", [P, RING])
        diag = sb("diag", [P, RING, P])
        key_s = sb("key_s", [P, HC, TOPK])
        key_i = sb("key_i", [P, HC, TOPK], U32)
        key_f = sb("key_f", [P, HC, TOPK])
        best_s = sb("best_s", [P, PH, TOPK])
        logits = sb("logits", [P, PH, TOPK])
        best_j = sb("best_j", [P, PH, TOPK], U32)
        row_j = sb("row_j", [P, 2, SLOTS], U32)
        row_f = sb("row_f", [P, 2, SLOTS])
        row_e = sb("row_e", [P, 2, SLOTS])
        gsum = sb("gsum", [P, 2, PH])
        work = sb("work", [P, 19500])

        def view(at, *shape):
            n = 1
            for d in shape:
                n *= d
            v = work[:, at:at + n]
            if len(shape) == 2:
                return v.rearrange("p (a b) -> p a b", a=shape[0])
            if len(shape) == 3:
                return v.rearrange("p (a b c) -> p a b c", a=shape[0], b=shape[1])
            return v

        conv = view(0, KC, S)
        squares = view(4096, KC, S)
        sig = view(8192, 2, S)
        hpad = view(8704, 2, PAD + S)
        acc_c = view(9300, 2, S)
        tap_c = view(9820, 2, W)
        ch_rstd = view(9900, 2, S)
        vec_raw = view(10500, P)
        taps_raw = view(10700, 4, P)
        bias_row = view(11300, D)
        q_chan = view(0, HC, S)
        score = view(4096, TB, HC * NKEY)
        pair_s = view(8192, PH, TOPK * TOPK)
        hot = view(10240, SLOTS, TOPK)
        sk_raw = view(16384, HC, P)
        sk_t = view(13400, HC, P)
        k_t = view(0, HEADS, S)
        v_tok = view(4096, TB, D)
        q_t = view(8192, HEADS, S)
        o_t = view(12288, HEADS, S)
        AW = S + P
        zc = view(16384, 2, AW)
        soft_a = view(16384 + 2 * AW, 2, AW)
        soft_b = view(16384 + 4 * AW, 2, AW)
        att = view(16384 + 6 * AW, 2, AW)

        consts = sem("consts")
        x_loaded, vec_loaded, bias_loaded = sem("x_loaded"), sem("vec_loaded"), sem("bias_loaded")
        rows_loaded, sk_loaded, stored = sem("rows_loaded"), sem("sk_loaded"), sem("stored")
        panel = [sem(f"panel{i}") for i in range(RING)]
        u_row = [sem(f"u_row{i}") for i in range(RING)]
        v_row = [sem(f"v_row{i}") for i in range(RING)]
        vec_t, vec_taken = sem("vec_t"), sem("vec_taken")
        xt_ready, xt_taken = sem("xt_ready"), sem("xt_taken")
        proj = sem("proj")
        chunk_taken = sem("chunk_taken")
        sig_ready = sem("sig_ready")
        glu_done = sem("glu_done")
        conv_steps = sem("conv_steps")
        ch_stat, ch_steps, ch_act = sem("ch_stat"), sem("ch_steps"), sem("ch_act")
        ln_steps = [sem(f"ln_steps{i}") for i in range(4)]
        ln_act = [sem(f"ln_act{i}") for i in range(4)]
        sk_ready, sk_taken = sem("sk_ready"), sem("sk_taken")
        score_ready, score_taken = sem("score_ready"), sem("score_taken")
        route = [sem(f"route{i}") for i in range(LAYERS)]
        route_exp = sem("route_exp")
        index_copied, pool_tick = sem("index_copied"), sem("pool_tick")
        u_used = sem("u_used")
        v_used = sem("v_used")
        gelu_done, coef_done, diag_done = sem("gelu_done"), sem("coef_done"), sem("diag_done")
        act_tick = sem("act_tick")
        v_taken = sem("v_taken")
        z_ready, rest_ready, o_ready = sem("z_ready"), sem("rest_ready"), sem("o_ready")
        z_abs, z_soft, z_logit, att_masked = sem("z_abs"), sem("z_soft"), sem("z_logit"), sem("att_masked")
        z_copied, z_log, att_exp, o_copied = sem("z_copied"), sem("z_log"), sem("att_exp"), sem("o_copied")

        u_tab = peer_u.rearrange("l e d -> (l e) d")
        v_tab = peer_v.rearrange("l e d -> (l e) d")

        def panel_chan(slot):
            return ring[:, slot, :].rearrange("p (c n) -> p c n", c=KC)

        def panel_tok(slot):
            return ring[:, slot, :].rearrange("p (c n) -> p c n", c=2)

        def row_tile(kind, i):
            return ring[:, 2 * kind + i // 2, (i % 2) * D:(i % 2 + 1) * D]

        def bank_cols(tb):
            return ps[:, Q * tb:Q * tb + Q, :].rearrange("p a b -> p (a b)")

        block = ctx.enter_context(nc.Block())

        @block.sync
        def _(sp):
            for tb in range(TB):
                sp.dma_start(x_tok[:, tb, :], x[0, tb * P:(tb + 1) * P, :]).then_inc(x_loaded, 16)

            def by_columns(w):
                return w.rearrange("(c p) n -> p c n", p=P)

            def load_chan(w, n, col, wait):
                if wait:
                    sp.wait_ge(proj, 2 * (n - RING + 1))
                sp.dma_start(panel_chan(n % RING), by_columns(w)[:, :, col:col + 256]).then_inc(panel[n % RING], 16)

            def load_tok(w, n, p):
                sp.wait_ge(proj, 2 * (n - RING + 1))
                sp.dma_start(panel_tok(n % RING), by_columns(w)[:, 2 * p:2 * p + 2, :]).then_inc(panel[n % RING], 16)

            def load_rows(n):
                if n:
                    sp.wait_ge(ln_steps[n - 1], TB * LN_STEPS)
                for i, w in enumerate((ln_g, ln_b)):
                    sp.dma_start(ln_rows[:, i, :], w[n // 2, n % 2:n % 2 + 1, :].partition_broadcast(P)) \
                      .then_inc(rows_loaded, 16)

            def load_keys(layer):
                sp.dma_start(sk_raw, peer_sub_keys[layer].rearrange("h c k d -> k (h c) d")).then_inc(sk_loaded, 16)

            w_in = conv_w_in[0]
            for n in range(RING):
                load_chan(w_in, n, (n % 2) * D + (n // 2) * 256, False)
                if n == 0:
                    sp.dma_start(vec_raw[0:NB_IN, :], conv_b_in.rearrange("l (r p) -> (l r) p", p=P)).then_inc(vec_loaded, 16)
                    for i, w in enumerate((conv_b_dw, conv_ln_g, conv_ln_b)):
                        at = NB_IN + i * KC
                        sp.dma_start(vec_raw[at:at + KC, :], w.rearrange("l (r p) -> (l r) p", p=P)).then_inc(vec_loaded, 16)
                    taps_by_row = conv_w_dw.rearrange("l w o (c p) -> (l w o c) p", p=P)
                    RT = W * KC // 4
                    sp.dma_start(taps_raw[0:RT, :, :], taps_by_row.rearrange("(r q) p -> q r p", q=RT)).then_inc(vec_loaded, 16)
            load_rows(0)
            sp.dma_start(bias_row[0:1, :], conv_b_out).then_inc(bias_loaded, 16)
            load_keys(0)
            with sp.Fori(1, 2 * PANELS // RING) as i:
                for s in range(RING):
                    sp.wait_ge(proj, 2 * RING * i + (2 * s - 2 * RING + 2))
                    sp.dma_start(panel_chan(s), by_columns(w_in)[:, :, bass.ds(i * 512 + ((s % 2) * D + (s // 2) * 256), 256)]) \
                      .then_inc(panel[s], 16)
            for p in range(PANELS):
                load_tok(conv_w_out[0], P_OUT + p, p)
            for p in range(PANELS):
                load_chan(peer_w_q[0], P_WQ[0] + p, p * 256, True)
            load_rows(1)
            for p in range(PANELS):
                if p == 0:
                    sp.wait_ge(u_used, RING + TB * SLOTS)
                if p == 2:
                    sp.wait_ge(v_used, RING + TB * SLOTS)
                load_chan(attn_w_kv, P_K + p, p * 256, True)
            load_rows(2)
            for p in range(PANELS):
                sp.wait_ge(proj, 2 * (P_V + p - RING + 1))
                sp.dma_start(panel_tok(p % RING), by_columns(attn_w_kv)[:, 2 * p:2 * p + 2, D:2 * D]).then_inc(panel[p % RING], 16)
            for p in range(PANELS):
                load_chan(attn_w_q[0], P_Q + p, p * 256, True)
            for p in range(PANELS):
                load_tok(attn_w_o[0], P_O + p, p)
                if p == RING - 1:
                    sp.wait_ge(o_copied, HEADS)
                    load_keys(1)
            for p in range(PANELS):
                load_chan(peer_w_q[1], P_WQ[1] + p, p * 256, True)
            load_rows(3)
            for tb in range(TB):
                sp.wait_ge(ln_steps[3], LN_STEPS * (tb + 1))
                sp.dma_start(out[0, tb * P:(tb + 1) * P, :], x_tok[:, tb, :]).then_inc(stored, 16)
            sp.wait_ge(stored, 16 * TB)

        @block.gpsimd
        def _(pool):
            pool.memset(ones[:, :], 1.0).then_inc(consts, 1)
            pool.memset(mean_ones[:, :], 1.0 / D).then_inc(consts, 1)
            pool.iota(iota_i[:, :], pattern=[[1, TOPK]], base=0, channel_multiplier=0).then_inc(consts, 1)
            pool.wait_ge(consts, 3)
            pool.affine_select(ident[:, :], ones[:, :], pattern=[[-1, P]], base=0, channel_multiplier=1,
                               compare_op=ALU.is_equal, fill=0.0).then_inc(consts, 1)
            pool.affine_select(tri[:, :], ones[:, :], pattern=[[-1, P]], base=0, channel_multiplier=1,
                               compare_op=ALU.is_ge, fill=0.0).then_inc(consts, 1)
            pool.affine_select(causal[:, :], ones[:, :], pattern=[[1, P]], base=0, channel_multiplier=-1,
                               compare_op=ALU.is_gt, fill=0.0).then_inc(consts, 1)
            pool.tensor_copy(iota_f[:, :], iota_i[:, :]).then_inc(consts, 1)
            pool.wait_ge(consts, 7)
            pool.tensor_scalar(alpha_ident[:, :], ident[:, :], ALPHA, None, ALU.mult).then_inc(consts, 1)

            for layer in range(LAYERS):
                for tb in range(TB):
                    pool.wait_ge(route[layer], ROUTE_STEPS * tb + ROUTE_INDEX)
                    if tb == 0:
                        pool.wait_ge(proj, 2 * (P_WQ[layer] + PANELS))
                    base = (layer * TB + tb) * GROUPS
                    with pool.Fori(0, GROUPS // 2) as i:
                        for half in range(2):
                            pool.tensor_copy(index_now[:, half, :],
                                             index[:, tb, bass.ds(i * (2 * RING) + half * RING, RING)]).then_inc(index_copied, 1)
                            pool.wait_ge(index_copied, i * 2 + (base + half + 1))
                            pool.sem_inc(pool_tick, 1)
                            pool.wait_ge(u_used, i * (2 * RING) + ((base + half) * RING + RING))
                            pool.sem_inc(pool_tick, 1)
                            for s in range(RING):
                                pool.indirect_dma_start(
                                    row_tile(0, s), None, u_tab,
                                    bass.IndirectOffsetOnAxis(ap=index_now[:, half, s:s + 1], axis=0)).then_inc(u_row[s], 16)
                            pool.wait_ge(v_used, i * (2 * RING) + ((base + half) * RING + RING))
                            pool.sem_inc(pool_tick, 1)
                            for s in range(RING):
                                pool.indirect_dma_start(
                                    row_tile(1, s), None, v_tab,
                                    bass.IndirectOffsetOnAxis(ap=index_now[:, half, s:s + 1], axis=0)).then_inc(v_row[s], 16)

        @block.tensor
        def _(pe):
            pe.sem_inc(v_used, RING)

            def turn_x(n):
                for tb in range(TB):
                    if n == 0:
                        pe.wait_ge(x_loaded, 16 * TB)
                        pe.wait_ge(vec_taken, 2)
                    else:
                        pe.wait_ge(ln_steps[n - 1], LN_STEPS * (tb + 1))
                    for j in range(KC // 4):
                        for c in range(4):
                            mm = pe.transpose(ps[:, Q * tb + j, c * P:(c + 1) * P],
                                              x_tok[:, tb, (4 * j + c) * P:(4 * j + c + 1) * P], ident[:, :])
                        mm.then_inc(xt_ready, 1)

            def project_chan(n0, taken0):
                with pe.Fori(0, PANELS // RING) as i:
                    for s in range(RING):
                        pe.wait_ge(panel[s], i * 16 + 16 * (n0 // RING + 1))
                        for m in range(2):
                            j = 2 * s + m
                            pe.wait_ge(chunk_taken, i * 8 + (taken0 + j + 1))
                            for k in range(KC):
                                mm = pe.matmul(ps[:, j, 0:S], panel_chan(s)[:, k, m * P:(m + 1) * P], x_chan[:, k, :],
                                               start=(k == 0), stop=(k == KC - 1))
                            mm.then_inc(proj, 1)

            def project_tok(n0, operand, first, ready):
                for p in range(PANELS):
                    n = n0 + p
                    pe.wait_ge(panel[n % RING], 16 * (n // RING + 1))
                    for kk in range(2):
                        k = 2 * p + kk
                        ready(k)
                        for tb in range(TB):
                            for q in range(Q):
                                mm = pe.matmul(ps[:, Q * tb + q, :], operand[:, k, tb * P:(tb + 1) * P],
                                               panel_tok(n % RING)[:, kk, q * 512:(q + 1) * 512],
                                               start=(first and k == 0), stop=(k == KC - 1), skip_group_check=True)
                    mm.then_inc(proj, 2)

            def residual(tb, q):
                return pe.matmul(ps[:, Q * tb + q, :], alpha_ident[:, :], x_tok[:, tb, q * 512:(q + 1) * 512],
                                 start=True, stop=True, skip_group_check=True)

            pe.wait_ge(consts, 8)
            pe.wait_ge(vec_loaded, 16 * 5)
            nv = NB_IN + 3 * KC
            pe.transpose(ps[:, 0, 0:nv], vec_raw[0:nv, :], ident[0:nv, 0:nv]).then_inc(vec_t, 1)
            RT = W * KC // 4
            for r in range(4):
                mm = pe.transpose(ps[:, 1, r * RT:(r + 1) * RT], taps_raw[0:RT, r, :], ident[0:RT, 0:RT])
            mm.then_inc(vec_t, 1)
            turn_x(0)

            pe.wait_ge(xt_taken, KC // 4 * TB)
            with pe.Fori(0, 2 * PANELS // RING) as i:
                for pair in range(2):
                    for kind in range(2):
                        s = 2 * pair + kind
                        pe.wait_ge(panel[s], i * 16 + 16)
                        for m in range(2):
                            bank = 2 * pair + m
                            if kind == 0:
                                pe.wait_ge(glu_done, i * 4 + (bank + 1))
                            for k in range(KC):
                                mm = pe.matmul(ps[:, bank, kind * S:(kind + 1) * S], panel_chan(s)[:, k, m * P:(m + 1) * P],
                                               x_chan[:, k, :], start=(k == 0), stop=(k == KC - 1))
                            mm.then_inc(proj, 1)

            def residual_bias(tb, q):
                residual(tb, q)
                pe.matmul(ps[:, Q * tb + q, :], ones[0:1, :], bias_row[0:1, q * 512:(q + 1) * 512],
                          start=False, stop=True, skip_group_check=True)

            pe.wait_ge(glu_done, 4 + KC)
            pe.wait_ge(bias_loaded, 16)
            for b in range(6):
                residual_bias(b // Q, b % Q)
            for k in range(KC):
                pe.wait_ge(conv_steps, (W + 1) * (k + 2))
                mm = pe.matmul(ps[:, 7, 0:S], mean_ones[:, :], conv[:, k, :], start=(k == 0), stop=(k == KC - 1))
            mm.then_inc(ch_stat, 1)
            for k in range(KC):
                pe.wait_ge(ch_act, k // 4 + 1)
                mm = pe.matmul(ps[:, 6, 0:S], mean_ones[:, :], squares[:, k, :], start=(k == 0), stop=(k == KC - 1))
            mm.then_inc(ch_stat, 1)
            pe.wait_ge(ch_steps, 5)
            residual_bias(1, 2)
            residual_bias(1, 3)
            project_tok(P_OUT, conv, False, lambda k: pe.wait_ge(ch_act, 6 + k))

            def peer(layer):
                turn_x(1 + 2 * layer)
                pe.wait_ge(sk_loaded, 16 * (layer + 1))
                for j in range(HC // 4):
                    pe.wait_ge(xt_taken, 8 * (1 + 2 * layer) + j + 1)
                    for c in range(4):
                        mm = pe.transpose(ps[:, j, c * P:(c + 1) * P], sk_raw[:, 4 * j + c, :], ident[:, :])
                    mm.then_inc(sk_ready, 1)
                pe.wait_ge(xt_taken, 8 * (2 + 2 * layer))
                pe.wait_ge(sk_taken, 4 * (layer + 1))
                project_chan(P_WQ[layer], 48 * layer)
                for tb in range(TB):
                    for hc in range(HC):
                        j = Q * tb + hc // 4
                        pe.wait_ge(chunk_taken, 8 + 48 * layer + (hc + 1 if hc >= 8 else KC))
                        mm = pe.matmul(ps[:, j, (hc % 4) * P:(hc % 4 + 1) * P], q_chan[:, hc, tb * P:(tb + 1) * P],
                                       sk_t[:, hc, :], start=True, stop=True)
                        if hc % 4 == 3:
                            mm.then_inc(score_ready, 1)
                for tb in range(TB):
                    pe.wait_ge(score_taken, 8 * layer + 4 * (tb + 1))
                    for q in range(Q):
                        residual(tb, q)
                    base = (layer * TB + tb) * GROUPS
                    with pe.Fori(0, GROUPS) as i:
                        for s in range(RING):
                            pe.wait_ge(diag_done, i * RING + (base * RING + s + 1))
                            pe.wait_ge(v_row[s], i * 16 + (base + 1) * 16)
                            for q in range(Q):
                                mm = pe.matmul(ps[:, Q * tb + q, :], diag[:, s, :], row_tile(1, s)[:, q * 512:(q + 1) * 512],
                                               start=False, stop=True, skip_group_check=True)
                            mm.then_inc(v_used, 1)

            peer(0)

            turn_x(2)
            pe.wait_ge(xt_taken, 24)
            project_chan(P_K, 16)
            pe.wait_ge(chunk_taken, 8 + 32)
            project_tok(P_V, x_chan, True, lambda k: None)
            pe.wait_ge(v_taken, 8)
            project_chan(P_Q, 32)
            pe.wait_ge(chunk_taken, 8 + 48)
            for it in range(HEADS + 2):
                if it < HEADS:
                    h = it
                    if h >= 2:
                        pe.wait_ge(z_copied, h - 1)
                        pe.wait_ge(z_soft, 2 * (h - 1))
                    pe.matmul(ps[:, h % 2, 0:S], k_t[:, h, 0:P], q_t[:, h, :], start=True, stop=True)
                    pe.matmul(ps[:, h % 2, S:AW], k_t[:, h, P:S], q_t[:, h, P:S], start=True, stop=True).then_inc(z_ready, 1)
                if 1 <= it <= HEADS:
                    h = it - 1
                    b = 2 + h % 2
                    pe.wait_ge(z_soft, 2 * (h + 1))
                    if h >= 2:
                        pe.wait_ge(z_logit, h - 1)
                    pe.matmul(ps[:, b, 0:S], tri[:, :], soft_b[:, h % 2, 0:S], start=True, stop=False, skip_group_check=True)
                    pe.matmul(ps[:, b, P:S], ones[:, :], soft_b[:, h % 2, S:AW], start=False, stop=True, skip_group_check=True)
                    pe.matmul(ps[:, b, S:AW], tri[:, :], soft_b[:, h % 2, S:AW], start=True, stop=True,
                              skip_group_check=True).then_inc(rest_ready, 1)
                if it >= 2:
                    h = it - 2
                    b = 4 + h % 2
                    pe.wait_ge(att_masked, h + 1)
                    if h >= 2:
                        pe.wait_ge(o_copied, h - 1)
                    pe.matmul(ps[:, b, 0:S], v_tok[:, 0, h * P:(h + 1) * P], att[:, h % 2, 0:S],
                              start=True, stop=False, skip_group_check=True)
                    pe.matmul(ps[:, b, P:S], v_tok[:, 1, h * P:(h + 1) * P], att[:, h % 2, S:AW],
                              start=False, stop=True, skip_group_check=True).then_inc(o_ready, 1)
            pe.wait_ge(o_copied, HEADS)
            for b in range(8):
                residual(b // Q, b % Q)
            project_tok(P_O, o_t, False, lambda k: None)
            peer(1)

        @block.scalar
        def _(act):
            act.sem_inc(chunk_taken, 8)

            def take_x(n):
                for b in range(8):
                    tb, j = b // Q, b % Q
                    act.wait_ge(xt_ready, 8 * n + b + 1)
                    act.activation(x_chan[:, 4 * j:4 * j + 4, tb * P:(tb + 1) * P],
                                   ps[:, b, :].rearrange("p (a b) -> p a b", a=4), ACT.Copy).then_inc(xt_taken, 1)

            def take_chunks(to, n0, scale):
                for j in range(KC):
                    act.wait_ge(proj, 2 * n0 + j + 1)
                    act.activation(to[:, j, :], ps[:, j % 8, 0:S], ACT.Copy, scale=scale).then_inc(chunk_taken, 1)

            def norm(n, tb):
                v = lnv[:, tb, :]
                act.wait_ge(ln_steps[n], LN_STEPS * tb + 6)
                act.activation(v[:, 1:2], v[:, 0:1], ACT.Sqrt).then_inc(ln_act[n], 1)
                act.wait_ge(ln_steps[n], LN_STEPS * tb + 8)
                act.activation(x_tok[:, tb, :], bank_cols(tb), ACT.Identity, scale=v[:, 2:3], bias=v[:, 3:4]).then_inc(ln_act[n], 1)

            act.wait_ge(vec_t, 1)
            act.activation(vec[:, :], ps[:, 0, 0:NB_IN + 3 * KC], ACT.Copy).then_inc(vec_taken, 1)
            act.wait_ge(vec_t, 2)
            act.activation(taps[:, :], ps[:, 1, 0:W * KC], ACT.Copy).then_inc(vec_taken, 1)
            take_x(0)
            act.wait_ge(vec_taken, 2)

            with act.Fori(0, KC // 4) as i:
                for b in range(4):
                    act.wait_ge(proj, i * 8 + (4 * (b // 2) + b % 2 + 3))
                    act.sem_inc(act_tick, 1)
                    act.wait_ge(glu_done, i * 4 + (b + 3))
                    act.sem_inc(act_tick, 1)
                    act.activation(sig[:, b % 2, :], ps[:, b, S:2 * S], ACT.Sigmoid,
                                   bias=vec[:, bass.ds(i * 4 + (KC + b), 1)]).then_inc(sig_ready, 1)

            for q in range(4):
                act.wait_ge(ch_steps, q + 1)
                act.activation(squares[:, 4 * q:4 * q + 4, :], conv[:, 4 * q:4 * q + 4, :], ACT.Square).then_inc(ch_act, 1)
            act.wait_ge(ch_steps, 5)
            act.activation(ch_rstd[:, 1, :], ch_rstd[:, 0, :], ACT.Sqrt).then_inc(ch_act, 1)
            for k in range(KC):
                act.wait_ge(ch_steps, 7 + k // 4)
                act.activation(conv[:, k, :], conv[:, k, :], ACT.Silu, scale=vec[:, NB_IN + KC + k:NB_IN + KC + k + 1],
                               bias=vec[:, NB_IN + 2 * KC + k:NB_IN + 2 * KC + k + 1]).then_inc(ch_act, 1)

            def peer(layer):
                for tb in range(TB):
                    norm(2 * layer, tb)
                take_x(1 + 2 * layer)
                for j in range(4):
                    act.wait_ge(sk_ready, 4 * layer + j + 1)
                    act.activation(sk_t[:, 4 * j:4 * j + 4, :], ps[:, j, :].rearrange("p (a b) -> p a b", a=4),
                                   ACT.Copy).then_inc(sk_taken, 1)
                take_chunks(q_chan, P_WQ[layer], 1.0)
                for b in range(8):
                    act.wait_ge(score_ready, 8 * layer + b + 1)
                    act.activation(score[:, b // Q, (b % Q) * 512:(b % Q + 1) * 512], ps[:, b, :], ACT.Copy).then_inc(score_taken, 1)
                for tb in range(TB):
                    act.wait_ge(route[layer], ROUTE_STEPS * tb + ROUTE_LOGITS)
                    act.activation(logits[:, :, :], logits[:, :, :], ACT.Exp).then_inc(route_exp, 1)
                for tb in range(TB):
                    base = (layer * TB + tb) * GROUPS
                    with act.Fori(0, GROUPS) as i:
                        act.wait_ge(u_used, i * RING + (base * RING + 2 * RING))
                        act.activation(gelu_now[:, :], h_now[:, :], ACT.Gelu).then_inc(gelu_done, 1)
                        act.wait_ge(coef_done, i + (base + 1))
                        for s in range(RING):
                            act.wait_ge(v_used, i * RING + (base * RING + s + 1))
                            act.activation(diag[:, s, :], ident[:, :], ACT.Copy, scale=coef_now[:, s:s + 1]).then_inc(diag_done, 1)
                    norm(2 * layer + 1, tb)

            peer(0)
            take_x(2)
            take_chunks(k_t, P_K, 1.0)
            act.wait_ge(proj, 2 * (P_V + PANELS))
            for b in range(8):
                act.activation(v_tok[:, b // Q, (b % Q) * 512:(b % Q + 1) * 512], ps[:, b, :], ACT.Copy).then_inc(v_taken, 1)
            take_chunks(q_t, P_Q, SCALE)
            act.preload_act_table_set("natural_log_exp_and_others")
            for it in range(HEADS + 2):
                if it < HEADS:
                    h = it
                    act.wait_ge(z_ready, h + 1)
                    if h >= 2:
                        act.wait_ge(z_logit, h - 1)
                    act.activation(zc[:, h % 2, :], ps[:, h % 2, 0:AW], ACT.Copy).then_inc(z_copied, 1)
                    act.wait_ge(z_abs, h + 1)
                    act.activation(soft_a[:, h % 2, :], soft_a[:, h % 2, :], ACT.Exp, scale=-1.0).then_inc(z_log, 1)
                    act.wait_ge(z_log, 2 * h + 1)
                    act.activation(soft_a[:, h % 2, :], soft_a[:, h % 2, :], ACT.Ln, bias=1.0).then_inc(z_log, 1)
                if 1 <= it <= HEADS:
                    h = it - 1
                    act.wait_ge(z_logit, h + 1)
                    if h >= 2:
                        act.wait_ge(o_ready, h - 1)
                    act.activation(att[:, h % 2, :], soft_a[:, h % 2, :], ACT.Exp).then_inc(att_exp, 1)
                if it >= 2:
                    h = it - 2
                    act.wait_ge(o_ready, h + 1)
                    act.activation(o_t[:, h, :], ps[:, 4 + h % 2, 0:S], ACT.Copy).then_inc(o_copied, 1)
            peer(1)

        @block.vector
        def _(dve):
            dve.sem_inc(u_used, RING)
            dve.sem_inc(glu_done, 4)

            dve.memset(hpad[:, :, 0:PAD], 0.0).then_inc(conv_steps, W + 1)
            dve.wait_ge(vec_taken, 2)
            taps_by = taps[:, :].rearrange("p (w c) -> p w c", c=KC)
            STEPS = W + 1
            with dve.Fori(0, KC // 4) as i:
                for b in range(4):
                    e = b % 2
                    at = (b + 1) * STEPS
                    dve.wait_ge(sig_ready, i * 4 + (b + 1))
                    dve.scalar_tensor_tensor(out=hpad[:, e, PAD:], in0=ps[:, b, 0:S], scalar=vec[:, bass.ds(i * 4 + b, 1)],
                                             in1=sig[:, e, :], op0=ALU.add, op1=ALU.mult).then_inc(glu_done, 1)
                    dve.tensor_copy(tap_c[:, e, :], taps_by[:, :, bass.ds(i * 4 + b, 1)].rearrange("p w c -> p (w c)")) \
                       .then_inc(conv_steps, 1)
                    dve.wait_ge(conv_steps, i * (4 * STEPS) + (at + 1))
                    dve.wait_ge(glu_done, i * 4 + (4 + b + 1))
                    dve.tensor_scalar(acc_c[:, e, :], hpad[:, e, 0:S], tap_c[:, e, 0:1],
                                      vec[:, bass.ds(i * 4 + (NB_IN + b), 1)], ALU.mult, ALU.add).then_inc(conv_steps, 1)
                    for w in range(1, W):
                        dve.wait_ge(conv_steps, i * (4 * STEPS) + (at + 1 + w))
                        to = acc_c[:, e, :] if w < W - 1 else conv[:, bass.ds(i * 4 + b, 1), :].rearrange("p a b -> p (a b)")
                        dve.scalar_tensor_tensor(out=to, in0=hpad[:, e, w:w + S], scalar=tap_c[:, e, w:w + 1],
                                                 in1=acc_c[:, e, :], op0=ALU.mult, op1=ALU.add).then_inc(conv_steps, 1)

            dve.wait_ge(ch_stat, 1)
            for q in range(4):
                c = conv[:, 4 * q:4 * q + 4, :]
                dve.tensor_tensor(out=c, in0=c, in1=ps[:, 7:8, 0:S].to_broadcast([P, 4, S]), op=ALU.subtract).then_inc(ch_steps, 1)
            dve.wait_ge(ch_stat, 2)
            dve.tensor_scalar(ch_rstd[:, 0, :], ps[:, 6, 0:S], LN_EPS, None, ALU.add).then_inc(ch_steps, 1)
            dve.wait_ge(ch_act, 5)
            dve.reciprocal(ch_rstd[:, 0, :], ch_rstd[:, 1, :]).then_inc(ch_steps, 1)
            dve.wait_ge(ch_steps, 6)
            for q in range(4):
                c = conv[:, 4 * q:4 * q + 4, :]
                dve.tensor_tensor(out=c, in0=c, in1=ch_rstd[:, 0:1, :].to_broadcast([P, 4, S]), op=ALU.mult).then_inc(ch_steps, 1)

            def norm(n, blocks):
                for tb in blocks:
                    at = LN_STEPS * tb
                    for q in range(Q):
                        dve.bn_stats(stats[:, tb, q, :], ps[:, Q * tb + q, :]).then_inc(ln_steps[n], 1)
                    dve.wait_ge(ln_steps[n], at + 4)
                    dve.bn_aggr(mv[:, tb, :], stats[:, tb, :, :]).then_inc(ln_steps[n], 1)
                    dve.wait_ge(ln_steps[n], at + 5)
                    dve.tensor_scalar(lnv[:, tb, 0:1], mv[:, tb, 1:2], LN_EPS, None, ALU.add).then_inc(ln_steps[n], 1)
                    dve.wait_ge(ln_act[n], 2 * tb + 1)
                    dve.reciprocal(lnv[:, tb, 2:3], lnv[:, tb, 1:2]).then_inc(ln_steps[n], 1)
                    dve.wait_ge(ln_steps[n], at + 7)
                    dve.scalar_tensor_tensor(out=lnv[:, tb, 3:4], in0=mv[:, tb, 0:1], scalar=-1.0, in1=lnv[:, tb, 2:3],
                                             op0=ALU.mult, op1=ALU.mult).then_inc(ln_steps[n], 1)
                    dve.wait_ge(ln_act[n], 2 * tb + 2)
                    dve.wait_ge(rows_loaded, 32 * (n + 1))
                    dve.tensor_tensor(out=x_tok[:, tb, :], in0=x_tok[:, tb, :], in1=ln_rows[:, 0, :], op=ALU.mult).then_inc(ln_steps[n], 1)
                    dve.wait_ge(ln_steps[n], at + 9)
                    dve.tensor_tensor(out=x_tok[:, tb, :], in0=x_tok[:, tb, :], in1=ln_rows[:, 1, :], op=ALU.add).then_inc(ln_steps[n], 1)

            def top16(values, indices, table, rows, at, done):
                for r in range(rows):
                    dve.max(values(r)[:, 0:8], table(r)).then_inc(done, 1)
                dve.wait_ge(done, at + rows)
                for r in range(rows):
                    dve.max_index(indices(r)[:, 0:8], values(r)[:, 0:8], table(r)).then_inc(done, 1)
                dve.wait_ge(done, at + 2 * rows)
                for r in range(rows):
                    dve.match_replace(table(r), values(r)[:, 0:8], table(r), -3.0e38).then_inc(done, 1)
                dve.wait_ge(done, at + 3 * rows)
                for r in range(rows):
                    dve.max(values(r)[:, 8:16], table(r)).then_inc(done, 1)
                dve.wait_ge(done, at + 4 * rows)
                for r in range(rows):
                    dve.max_index(indices(r)[:, 8:16], values(r)[:, 8:16], table(r)).then_inc(done, 1)
                dve.wait_ge(done, at + 5 * rows)

            def routing(layer, tb):
                done = route[layer]
                at = ROUTE_STEPS * tb
                dve.wait_ge(score_taken, 8 * layer + 4 * (tb + 1))
                top16(lambda r: key_s[:, r, :], lambda r: key_i[:, r, :],
                      lambda r: score[:, tb, r * NKEY:(r + 1) * NKEY], HC, at, done)
                halves = key_s[:, :, :].rearrange("p (h c) k -> p h c k", c=2)
                dve.tensor_tensor(out=pair_s[:, :, :].rearrange("p h (a b) -> p h a b", a=TOPK),
                                  in0=halves[:, :, 0, :].unsqueeze(3).to_broadcast([P, PH, TOPK, TOPK]),
                                  in1=halves[:, :, 1, :].unsqueeze(2).to_broadcast([P, PH, TOPK, TOPK]),
                                  op=ALU.add).then_inc(done, 1)
                dve.wait_ge(done, at + 81)
                top16(lambda r: best_s[:, r, :], lambda r: best_j[:, r, :], lambda r: pair_s[:, r, :], PH, at + 81, done)
                dve.tensor_tensor(out=logits[:, :, :], in0=best_s[:, :, :],
                                  in1=best_s[:, :, 0:1].to_broadcast([P, PH, TOPK]), op=ALU.subtract).then_inc(done, 1)
                flat_j = best_j[:, :, :].rearrange("p h k -> p (h k)")
                dve.tensor_scalar(row_j[:, 0, :], flat_j, 4, None, ALU.logical_shift_right).then_inc(done, 1)
                dve.tensor_scalar(row_j[:, 1, :], flat_j, TOPK - 1, None, ALU.bitwise_and).then_inc(done, 1)
                dve.wait_ge(done, at + 124)
                dve.tensor_copy(row_f[:, 0, :], row_j[:, 0, :]).then_inc(done, 1)
                dve.tensor_copy(row_f[:, 1, :], row_j[:, 1, :]).then_inc(done, 1)
                dve.tensor_copy(key_f[:, :, :], key_i[:, :, :]).then_inc(done, 1)
                dve.wait_ge(done, at + 127)
                keys = key_f[:, :, :].rearrange("p (h c) k -> p h c k", c=2)
                hot_hk = hot[:, :, :].rearrange("p (h k) a -> p h k a", h=PH)
                for c in range(2):
                    dve.tensor_tensor(out=hot[:, :, :], in0=row_f[:, c, :].unsqueeze(2).to_broadcast([P, SLOTS, TOPK]),
                                      in1=iota_f[:, :].unsqueeze(1).to_broadcast([P, SLOTS, TOPK]), op=ALU.is_equal).then_inc(done, 1)
                    dve.wait_ge(done, at + 128 + 3 * c)
                    dve.tensor_tensor(out=hot_hk, in0=hot_hk, in1=keys[:, :, c, :].unsqueeze(2).to_broadcast([P, PH, TOPK, TOPK]),
                                      op=ALU.mult).then_inc(done, 1)
                    dve.wait_ge(done, at + 129 + 3 * c)
                    dve.tensor_reduce(row_e[:, c, :], hot[:, :, :], AX_X, ALU.add).then_inc(done, 1)
                    dve.wait_ge(done, at + 130 + 3 * c)
                dve.scalar_tensor_tensor(out=row_e[:, 0, :], in0=row_e[:, 0, :], scalar=float(NKEY), in1=row_e[:, 1, :],
                                         op0=ALU.mult, op1=ALU.add).then_inc(done, 1)
                dve.wait_ge(done, at + 134)
                dve.tensor_scalar(index[:, tb, :], row_e[:, 0, :], float(layer * NEXP), None, ALU.add).then_inc(done, 1)
                dve.wait_ge(route_exp, TB * layer + tb + 1)
                dve.tensor_reduce(gsum[:, 0, :], logits[:, :, :], AX_X, ALU.add).then_inc(done, 1)
                dve.wait_ge(done, at + 136)
                dve.reciprocal(gsum[:, 1, :], gsum[:, 0, :]).then_inc(done, 1)
                dve.wait_ge(done, at + 137)
                dve.tensor_tensor(out=gate[:, tb, :].rearrange("p (h k) -> p h k", k=TOPK), in0=logits[:, :, :],
                                  in1=gsum[:, 1, :].unsqueeze(2).to_broadcast([P, PH, TOPK]), op=ALU.mult).then_inc(done, 1)
                dve.wait_ge(done, at + 138)

            def peer(layer):
                dve.wait_ge(proj, 2 * (P_WQ[layer]))
                norm(2 * layer, range(TB))
                for tb in range(TB):
                    routing(layer, tb)
                for tb in range(TB):
                    base = (layer * TB + tb) * GROUPS
                    with dve.Fori(0, GROUPS) as i:
                        for s in range(RING):
                            dve.wait_ge(u_row[s], i * 16 + (base + 1) * 16)
                            dve.scalar_tensor_tensor(out=row_tile(0, s), in0=row_tile(0, s), scalar=1.0, in1=x_tok[:, tb, :],
                                                     op0=ALU.mult, op1=ALU.mult, accum_out=h_now[:, s:s + 1]).then_inc(u_used, 1)
                        if layer or tb:
                            dve.wait_ge(diag_done, i * RING + base * RING)
                        dve.wait_ge(gelu_done, i + (base + 1))
                        dve.tensor_tensor(out=coef_now[:, :], in0=gelu_now[:, :], in1=gate[:, tb, bass.ds(i * RING, RING)],
                                          op=ALU.mult).then_inc(coef_done, 1)
                    dve.wait_ge(v_used, RING + (base + GROUPS) * RING)
                    norm(2 * layer + 1, [tb])

            peer(0)

            for it in range(HEADS + 1):
                if it < HEADS:
                    h = it
                    e = h % 2
                    z = ps[:, e, 0:AW]
                    dve.wait_ge(z_copied, h + 1)
                    if h >= 2:
                        dve.wait_ge(att_exp, h - 1)
                    dve.scalar_tensor_tensor(out=soft_a[:, e, :], in0=z, scalar=-1.0, in1=zc[:, e, :],
                                             op0=ALU.mult, op1=ALU.max).then_inc(z_abs, 1)
                    dve.wait_ge(z_log, 2 * h + 2)
                    if h >= 2:
                        dve.wait_ge(rest_ready, h - 1)
                    dve.scalar_tensor_tensor(out=soft_b[:, e, :], in0=z, scalar=0.0, in1=soft_a[:, e, :],
                                             op0=ALU.max, op1=ALU.add).then_inc(z_soft, 1)
                    dve.wait_ge(z_soft, 2 * h + 1)
                    diagonal = soft_b[:, e, :].rearrange("p (a b) -> p a b", b=P)[:, 0:3:2, :]
                    dve.tensor_tensor(out=diagonal, in0=diagonal, in1=causal[:, :].unsqueeze(1).to_broadcast([P, 2, P]),
                                      op=ALU.mult).then_inc(z_soft, 1)
                if it >= 1:
                    h = it - 1
                    e = h % 2
                    dve.wait_ge(rest_ready, h + 1)
                    dve.wait_ge(z_copied, h + 1)
                    dve.tensor_tensor(out=soft_a[:, e, :], in0=zc[:, e, :], in1=ps[:, 2 + e, 0:AW], op=ALU.subtract).then_inc(z_logit, 1)
                    dve.wait_ge(att_exp, h + 1)
                    diagonal = att[:, e, :].rearrange("p (a b) -> p a b", b=P)[:, 0:3:2, :]
                    dve.scalar_tensor_tensor(out=diagonal, in0=diagonal, scalar=1.0,
                                             in1=causal[:, :].unsqueeze(1).to_broadcast([P, 2, P]),
                                             op0=ALU.min, op1=ALU.mult).then_inc(att_masked, 1)
            peer(1)


_INS = ["x", "conv_w_in", "conv_b_in", "conv_w_dw", "conv_b_dw", "conv_ln_g", "conv_ln_b", "conv_w_out", "conv_b_out",
        "attn_w_kv", "attn_w_q", "attn_w_o", "peer_w_q", "peer_sub_keys", "peer_u", "peer_v", "ln_g", "ln_b"]


def kernel(**inputs):
    import numpy as np
    import concourse.bacc as bacc
    from concourse.bass_utils import run_bass_kernel_spmd

    nc = bacc.Bacc("TRN2", target_bir_lowering=False, num_devices=1)
    arrays, args = {}, []
    for name in _INS:
        a = np.ascontiguousarray(inputs[name])
        arrays[f"in_{name}"] = a
        args.append(nc.dram_tensor(f"in_{name}", a.shape, mybir.dt.from_np(a.dtype), kind="ExternalInput").ap())
    out = nc.dram_tensor("out_dram", inputs["x"].shape, F32, kind="ExternalOutput").ap()
    build(nc, *args, out)
    r = run_bass_kernel_spmd(nc, [arrays], core_ids=[0])
    return r.results[0]["out_dram"]
```

```python
from contextlib import ExitStack

import concourse.bass as bass
from concourse import mybir

F32 = mybir.dt.float32
F32R = mybir.dt.float32r
U32 = mybir.dt.uint32
ALU = mybir.AluOpType
ACT = mybir.ActivationFunctionType
AX_X = mybir.AxisListType.X

P = 128
LN_EPS = 1e-5
TOPK = 16
RING = 4
LN_STEPS = 10
HEAD_STEPS = 31
PART_LOGITS = 1
PART_INDEX = 14
PART_STEPS = 17
EARLY_HEADS = 6


def build(nc, x, conv_w_in, conv_b_in, conv_w_dw, conv_b_dw, conv_ln_g, conv_ln_b, conv_w_out, conv_b_out,
          attn_w_kv, attn_w_q, attn_w_o, peer_w_q, peer_sub_keys, peer_u, peer_v, ln_g, ln_b, out):
    _, S, D = x.shape
    KC = D // P
    TB = S // P
    W = conv_w_dw.shape[1]
    PAD = W - 1
    HEADS = D // P
    LAYERS, PH, _, NKEY, DQ = peer_sub_keys.shape
    HC = PH * 2
    NEXP = peer_u.shape[1]
    SLOTS = PH * TOPK
    GROUPS = SLOTS // RING
    ALPHA = (2.0 * LAYERS) ** 0.25
    SCALE = float(P) ** -0.5

    def head_at(h):
        return HEAD_STEPS * h + (PART_STEPS if h >= EARLY_HEADS else 0)

    def part_at(tb, half):
        n = 2 * tb + half
        return HEAD_STEPS * (PH if n else EARLY_HEADS) + PART_STEPS * n
    Q = D // 512
    PANELS = 8
    assert TB == 2 and KC == 16 and Q == 4 and NKEY == P and DQ == P and HC == KC

    P_OUT, P_WQ = 2 * PANELS, [3 * PANELS, 8 * PANELS]
    HALVES = 2 * PANELS
    P_K, P_V, P_Q, P_O = 4 * PANELS, 5 * PANELS, 6 * PANELS, 7 * PANELS

    with ExitStack() as ctx:
        def sb(name, shape, dt=F32):
            return ctx.enter_context(nc.sbuf_tensor(name, shape, dt))

        def sem(name):
            return ctx.enter_context(nc.semaphore(name))

        ps = ctx.enter_context(nc.psum_tensor("ps", [P, 8, 512], F32))
        x_tok = sb("x_tok", [P, TB, D])
        x_chan_at = nc.sbuf_base
        x_chan = sb("x_chan", [P, KC, S])
        ring_at = nc.sbuf_base
        ring = sb("ring", [P, RING, 2 * D])
        ln_rows = sb("ln_rows", [P, 2, D])
        ident = sb("ident", [P, P])
        alpha_ident = sb("alpha_ident", [P, P])
        ones = sb("ones", [P, P])
        mean_ones = sb("mean_ones", [P, P])
        tri = sb("tri", [P, P])
        causal = sb("causal", [P, P])
        iota_i = sb("iota_i", [P, TOPK], mybir.dt.int32)
        iota_f = sb("iota_f", [P, TOPK])
        NB_IN = 2 * KC
        vec = sb("vec", [P, NB_IN + 3 * KC])
        taps = sb("taps", [P, W * KC])
        stats = sb("stats", [P, TB, Q, 6])
        mv = sb("mv", [P, TB, 2])
        lnv = sb("lnv", [P, TB, 4])
        index = sb("index", [P, TB, SLOTS], U32)
        gate = sb("gate", [P, TB, SLOTS])
        index_now = sb("index_now", [P, 2, RING], U32)
        h_now = sb("h_now", [P, RING])
        gelu_now = sb("gelu_now", [P, RING])
        coef_now = sb("coef_now", [P, RING])
        diag = sb("diag", [P, RING, P])
        logits = sb("logits", [P, PH, TOPK])
        row_j = sb("row_j", [P, 2, SLOTS], U32)
        row_f = sb("row_f", [P, 2, SLOTS])
        row_e = sb("row_e", [P, 2, SLOTS])
        gsum = sb("gsum", [P, 2, PH])
        work_at = nc.sbuf_base
        work = sb("work", [P, 19500])
        x_hi = nc.alloc_sbuf_tensor_at("x_hi", [P, KC, S], F32R, offset=x_chan_at)
        x_lo = nc.alloc_sbuf_tensor_at("x_lo", [P, KC, S], F32R, offset=work_at + 4 * 12288)
        w_hi = nc.alloc_sbuf_tensor_at("w_hi", [P, 2, D], F32R, offset=ring_at + 4 * 2 * 2 * D)
        w_lo = nc.alloc_sbuf_tensor_at("w_lo", [P, 2, D], F32R, offset=ring_at + 4 * 3 * 2 * D)

        def view(at, *shape):
            n = 1
            for d in shape:
                n *= d
            v = work[:, at:at + n]
            if len(shape) == 2:
                return v.rearrange("p (a b) -> p a b", a=shape[0])
            if len(shape) == 3:
                return v.rearrange("p (a b c) -> p a b c", a=shape[0], b=shape[1])
            return v

        conv = view(0, KC, S)
        squares = view(4096, KC, S)
        sig = view(8192, 2, S)
        hpad = view(8704, 2, PAD + S)
        acc_c = view(9300, 2, S)
        tap_c = view(9820, 2, W)
        ch_rstd = view(9900, 2, S)
        vec_raw = view(10500, P)
        taps_raw = view(10700, 4, P)
        bias_row = view(11300, D)
        q_now = view(0, 8, S)
        key_s = view(2048, TB, HC, TOPK)
        key_i = view(2560, TB, HC, TOPK).bitcast(U32)
        key_f = view(3072, HC, TOPK)
        best_s = view(3328, TB, PH, TOPK)
        best_j = view(3584, TB, PH, TOPK).bitcast(U32)
        score = view(4096, TB, HC * NKEY)
        pair_s = view(8192, TB, TOPK * TOPK)
        hot = view(10240, SLOTS, TOPK)
        sk_raw = view(16384, HC, P)
        sk_t = view(13400, HC, P)
        k_t = view(0, HEADS, S)
        v_tok = view(4096, TB, D)
        q_t = view(8192, HEADS, S)
        o_t = view(12288, HEADS, S)
        AW = S + P
        zc = view(16384, 2, AW)
        soft_a = view(16384 + 2 * AW, 2, AW)
        soft_b = view(16384 + 4 * AW, 2, AW)
        att = view(16384 + 6 * AW, 2, AW)

        consts = sem("consts")
        x_loaded, vec_loaded, bias_loaded = sem("x_loaded"), sem("vec_loaded"), sem("bias_loaded")
        rows_loaded, sk_loaded, stored = sem("rows_loaded"), sem("sk_loaded"), sem("stored")
        panel = [sem(f"panel{i}") for i in range(RING)]
        u_row = [sem(f"u_row{i}") for i in range(RING)]
        v_row = [sem(f"v_row{i}") for i in range(RING)]
        vec_t, vec_taken = sem("vec_t"), sem("vec_taken")
        xt_ready, xt_taken = sem("xt_ready"), sem("xt_taken")
        first_sum = sem("first_sum")
        x_split = sem("x_split")
        w_rounded, w_split = sem("w_rounded"), sem("w_split")
        proj = sem("proj")
        chunk_taken = sem("chunk_taken")
        sig_ready = sem("sig_ready")
        glu_done = sem("glu_done")
        conv_steps = sem("conv_steps")
        ch_stat, ch_steps, ch_act = sem("ch_stat"), sem("ch_steps"), sem("ch_act")
        ln_steps = [sem(f"ln_steps{i}") for i in range(4)]
        ln_act = [sem(f"ln_act{i}") for i in range(4)]
        sk_ready, sk_taken = sem("sk_ready"), sem("sk_taken")
        score_ready = sem("score_ready")
        score_taken = sem("score_taken")
        route = [sem(f"route{i}") for i in range(LAYERS)]
        route_exp = sem("route_exp")
        index_copied, pool_tick = sem("index_copied"), sem("pool_tick")
        u_used = sem("u_used")
        v_used = sem("v_used")
        gelu_done, coef_done, diag_done = sem("gelu_done"), sem("coef_done"), sem("diag_done")
        act_tick = sem("act_tick")
        v_taken = sem("v_taken")
        z_ready, rest_ready, o_ready = sem("z_ready"), sem("rest_ready"), sem("o_ready")
        z_abs, z_soft, z_logit, att_masked = sem("z_abs"), sem("z_soft"), sem("z_logit"), sem("att_masked")
        z_copied, z_log, att_exp, o_copied = sem("z_copied"), sem("z_log"), sem("att_exp"), sem("o_copied")

        u_tab = peer_u.rearrange("l e d -> (l e) d")
        v_tab = peer_v.rearrange("l e d -> (l e) d")

        def panel_chan(slot):
            return ring[:, slot, :].rearrange("p (c n) -> p c n", c=KC)

        def panel_tok(slot):
            return ring[:, slot, :].rearrange("p (c n) -> p c n", c=2)

        def landed(n):
            if n < P_K:
                return n // RING + 1
            if n < P_O:
                return P_K // RING + (n - P_K) // 2 + 1
            return P_K // RING + (n - P_O) // RING + 1 + ((P_O - P_K) // 2 if n % RING < 2 else 0)

        def raw_half(u):
            slot, m = (u // 2) % 2, u % 2
            if HALVES <= u < 2 * HALVES:
                return panel_tok(slot)[:, m, :]
            return panel_chan(slot)[:, :, m * P:(m + 1) * P]

        def half_as(buf, u):
            v = buf[:, u % 2, :]
            return v if HALVES <= u < 2 * HALVES else v.rearrange("p (c n) -> p c n", c=KC)

        def row_tile(kind, i):
            return ring[:, 2 * kind + i // 2, (i % 2) * D:(i % 2 + 1) * D]

        def bank_cols(tb):
            return ps[:, Q * tb:Q * tb + Q, :].rearrange("p a b -> p (a b)")

        block = ctx.enter_context(nc.Block())

        @block.sync
        def _(sp):
            for tb in range(TB):
                sp.dma_start(x_tok[:, tb, :], x[0, tb * P:(tb + 1) * P, :]).then_inc(x_loaded, 16)

            def by_columns(w):
                return w.rearrange("(c p) n -> p c n", p=P)

            def load_chan(w, n, col, wait):
                if wait:
                    sp.wait_ge(proj, 2 * (n - RING + 1))
                sp.dma_start(panel_chan(n % RING), by_columns(w)[:, :, col:col + 256]).then_inc(panel[n % RING], 16)

            def load_tok(w, n, p):
                sp.wait_ge(proj, 2 * (n - RING + 1))
                sp.dma_start(panel_tok(n % RING), by_columns(w)[:, 2 * p:2 * p + 2, :]).then_inc(panel[n % RING], 16)

            def load_rows(n):
                if n:
                    sp.wait_ge(ln_steps[n - 1], TB * LN_STEPS)
                for i, w in enumerate((ln_g, ln_b)):
                    sp.dma_start(ln_rows[:, i, :], w[n // 2, n % 2:n % 2 + 1, :].partition_broadcast(P)) \
                      .then_inc(rows_loaded, 16)

            def load_keys(layer):
                sp.dma_start(sk_raw, peer_sub_keys[layer].rearrange("h c k d -> k (h c) d")).then_inc(sk_loaded, 16)

            w_in = conv_w_in[0]
            for n in range(RING):
                load_chan(w_in, n, (n % 2) * D + (n // 2) * 256, False)
                if n == 0:
                    sp.dma_start(vec_raw[0:NB_IN, :], conv_b_in.rearrange("l (r p) -> (l r) p", p=P)).then_inc(vec_loaded, 16)
                    for i, w in enumerate((conv_b_dw, conv_ln_g, conv_ln_b)):
                        at = NB_IN + i * KC
                        sp.dma_start(vec_raw[at:at + KC, :], w.rearrange("l (r p) -> (l r) p", p=P)).then_inc(vec_loaded, 16)
                    taps_by_row = conv_w_dw.rearrange("l w o (c p) -> (l w o c) p", p=P)
                    RT = W * KC // 4
                    sp.dma_start(taps_raw[0:RT, :, :], taps_by_row.rearrange("(r q) p -> q r p", q=RT)).then_inc(vec_loaded, 16)
            load_rows(0)
            sp.dma_start(bias_row[0:1, :], conv_b_out).then_inc(bias_loaded, 16)
            load_keys(0)
            with sp.Fori(1, 2 * PANELS // RING) as i:
                for s in range(RING):
                    sp.wait_ge(proj, 2 * RING * i + (2 * s - 2 * RING + 2))
                    sp.dma_start(panel_chan(s), by_columns(w_in)[:, :, bass.ds(i * 512 + ((s % 2) * D + (s // 2) * 256), 256)]) \
                      .then_inc(panel[s], 16)
            for p in range(PANELS):
                load_tok(conv_w_out[0], P_OUT + p, p)
            for p in range(PANELS):
                load_chan(peer_w_q[0], P_WQ[0] + p, p * 256, True)
            load_rows(1)
            def load_split(w, n, token_major, at):
                local = n - P_K
                if local >= 2:
                    sp.wait_ge(w_split, 2 * (local - 1))
                if token_major:
                    to, src = panel_tok(local % 2), by_columns(w)[:, 2 * at:2 * at + 2, D:2 * D]
                else:
                    to, src = panel_chan(local % 2), by_columns(w)[:, :, at * 256:at * 256 + 256]
                sp.dma_start(to, src).then_inc(panel[local % 2], 16)

            sp.wait_ge(u_used, RING + TB * SLOTS)
            for p in range(PANELS):
                load_split(attn_w_kv, P_K + p, False, p)
            load_rows(2)
            for p in range(PANELS):
                load_split(attn_w_kv, P_V + p, True, p)
            for p in range(PANELS):
                load_split(attn_w_q[0], P_Q + p, False, p)
            for p in range(PANELS):
                if p == 0:
                    sp.wait_ge(w_split, 3 * HALVES)
                if p == 2:
                    sp.wait_ge(proj, 2 * P_O)
                if p < RING:
                    sp.dma_start(panel_tok(p), by_columns(attn_w_o[0])[:, 2 * p:2 * p + 2, :]).then_inc(panel[p], 16)
                else:
                    load_tok(attn_w_o[0], P_O + p, p)
                if p == RING - 1:
                    sp.wait_ge(o_copied, HEADS)
                    load_keys(1)
            for p in range(PANELS):
                load_chan(peer_w_q[1], P_WQ[1] + p, p * 256, True)
            load_rows(3)
            for tb in range(TB):
                sp.wait_ge(ln_steps[3], LN_STEPS * (tb + 1))
                sp.dma_start(out[0, tb * P:(tb + 1) * P, :], x_tok[:, tb, :]).then_inc(stored, 16)
            sp.wait_ge(stored, 16 * TB)

        @block.gpsimd
        def _(pool):
            pool.memset(ones[:, :], 1.0).then_inc(consts, 1)
            pool.memset(mean_ones[:, :], 1.0 / D).then_inc(consts, 1)
            pool.iota(iota_i[:, :], pattern=[[1, TOPK]], base=0, channel_multiplier=0).then_inc(consts, 1)
            pool.wait_ge(consts, 3)
            pool.affine_select(ident[:, :], ones[:, :], pattern=[[-1, P]], base=0, channel_multiplier=1,
                               compare_op=ALU.is_equal, fill=0.0).then_inc(consts, 1)
            pool.affine_select(tri[:, :], ones[:, :], pattern=[[-1, P]], base=0, channel_multiplier=1,
                               compare_op=ALU.is_ge, fill=0.0).then_inc(consts, 1)
            pool.affine_select(causal[:, :], ones[:, :], pattern=[[1, P]], base=0, channel_multiplier=-1,
                               compare_op=ALU.is_gt, fill=0.0).then_inc(consts, 1)
            pool.tensor_copy(iota_f[:, :], iota_i[:, :]).then_inc(consts, 1)
            pool.wait_ge(consts, 7)
            pool.tensor_scalar(alpha_ident[:, :], ident[:, :], ALPHA, None, ALU.mult).then_inc(consts, 1)

            for layer in range(LAYERS):
                for tb in range(TB):
                    if tb == 0:
                        pool.wait_ge(proj, 2 * (P_WQ[layer] + PANELS))
                    for part in range(2):
                        pool.wait_ge(route[layer], part_at(tb, part) + PART_INDEX)
                        base = (layer * TB + tb) * GROUPS + part * (GROUPS // 2)
                        with pool.Fori(0, GROUPS // 4) as i:
                            for half in range(2):
                                pool.tensor_copy(index_now[:, half, :],
                                                 index[:, tb, bass.ds(i * (2 * RING) + (part * (SLOTS // 2) + half * RING), RING)]) \
                                    .then_inc(index_copied, 1)
                                pool.wait_ge(index_copied, i * 2 + (base + half + 1))
                                pool.sem_inc(pool_tick, 1)
                                pool.wait_ge(u_used, i * (2 * RING) + ((base + half) * RING + RING))
                                pool.sem_inc(pool_tick, 1)
                                for s in range(RING):
                                    pool.indirect_dma_start(
                                        row_tile(0, s), None, u_tab,
                                        bass.IndirectOffsetOnAxis(ap=index_now[:, half, s:s + 1], axis=0)).then_inc(u_row[s], 16)
                                pool.wait_ge(v_used, i * (2 * RING) + ((base + half) * RING + RING))
                                pool.sem_inc(pool_tick, 1)
                                for s in range(RING):
                                    pool.indirect_dma_start(
                                        row_tile(1, s), None, v_tab,
                                        bass.IndirectOffsetOnAxis(ap=index_now[:, half, s:s + 1], axis=0)).then_inc(v_row[s], 16)

        @block.tensor
        def _(pe):
            pe.sem_inc(v_used, RING)

            def turn_x(n):
                for tb in range(TB):
                    if n == 0:
                        pe.wait_ge(x_loaded, 16 * TB)
                        pe.wait_ge(vec_taken, 2)
                    else:
                        pe.wait_ge(ln_steps[n - 1], LN_STEPS * (tb + 1))
                    for j in range(KC // 4):
                        for c in range(4):
                            mm = pe.transpose(ps[:, Q * tb + j, c * P:(c + 1) * P],
                                              x_tok[:, tb, (4 * j + c) * P:(4 * j + c + 1) * P], ident[:, :])
                        mm.then_inc(xt_ready, 1)

            def passes(k, u, cols, x_cols):
                for w, xx in ((w_hi, x_hi), (w_hi, x_lo), (w_lo, x_hi)):
                    yield half_as(w, u)[:, k, cols] if cols is not None else half_as(w, u), xx[:, k, x_cols]

            def split_chan(u0, taken0):
                with pe.Fori(0, HALVES // 8) as i:
                    for j in range(8):
                        u = u0 + j
                        pe.wait_ge(w_split, i * 8 + (u + 1))
                        pe.wait_ge(chunk_taken, i * 8 + (taken0 + j + 1))
                        for k in range(KC):
                            for t, (w, xx) in enumerate(passes(k, u, slice(0, P), slice(0, S))):
                                mm = pe.matmul(ps[:, j, 0:S], w, xx, start=(k == 0 and t == 0), stop=(k == KC - 1 and t == 2))
                        mm.then_inc(proj, 1)

            def split_tok(u0):
                for k in range(KC):
                    u = u0 + k
                    pe.wait_ge(w_split, u + 1)
                    for tb in range(TB):
                        for q in range(Q):
                            for t, (w, xx) in enumerate(passes(k, u, None, slice(tb * P, (tb + 1) * P))):
                                mm = pe.matmul(ps[:, Q * tb + q, :], xx, w[:, q * 512:(q + 1) * 512],
                                               start=(k == 0 and t == 0), stop=(k == KC - 1 and t == 2), skip_group_check=True)
                        if k == KC - 1 and tb == 0:
                            mm.then_inc(first_sum, 1)
                    mm.then_inc(proj, 1)

            def project_tok(n0, operand, ready):
                def multiply(p, blocks):
                    n = n0 + p
                    for kk in range(2):
                        k = 2 * p + kk
                        for tb in blocks:
                            if tb == 0:
                                ready(k)
                            for q in range(Q):
                                mm = pe.matmul(ps[:, Q * tb + q, :], operand[:, k, tb * P:(tb + 1) * P],
                                               panel_tok(n % RING)[:, kk, q * 512:(q + 1) * 512],
                                               start=False, stop=(k == KC - 1), skip_group_check=True)
                    return mm

                for p in range(PANELS - RING):
                    pe.wait_ge(panel[(n0 + p) % RING], 16 * landed(n0 + p))
                    multiply(p, range(TB)).then_inc(proj, 2)
                for p in range(PANELS - RING, PANELS):
                    pe.wait_ge(panel[(n0 + p) % RING], 16 * landed(n0 + p))
                    mm = multiply(p, [0])
                mm.then_inc(first_sum, 1)
                for p in range(PANELS - RING, PANELS):
                    multiply(p, [1]).then_inc(proj, 2)

            def residual(tb, q):
                return pe.matmul(ps[:, Q * tb + q, :], alpha_ident[:, :], x_tok[:, tb, q * 512:(q + 1) * 512],
                                 start=True, stop=True, skip_group_check=True)

            pe.wait_ge(consts, 8)
            pe.wait_ge(vec_loaded, 16 * 5)
            nv = NB_IN + 3 * KC
            pe.transpose(ps[:, 0, 0:nv], vec_raw[0:nv, :], ident[0:nv, 0:nv]).then_inc(vec_t, 1)
            RT = W * KC // 4
            for r in range(4):
                mm = pe.transpose(ps[:, 1, r * RT:(r + 1) * RT], taps_raw[0:RT, r, :], ident[0:RT, 0:RT])
            mm.then_inc(vec_t, 1)
            turn_x(0)

            pe.wait_ge(xt_taken, KC // 4 * TB)
            with pe.Fori(0, 2 * PANELS // RING) as i:
                for pair in range(2):
                    for kind in range(2):
                        s = 2 * pair + kind
                        pe.wait_ge(panel[s], i * 16 + 16)
                        for m in range(2):
                            bank = 2 * pair + m
                            if kind == 0:
                                pe.wait_ge(glu_done, i * 4 + (bank + 1))
                            for k in range(KC):
                                mm = pe.matmul(ps[:, bank, kind * S:(kind + 1) * S], panel_chan(s)[:, k, m * P:(m + 1) * P],
                                               x_chan[:, k, :], start=(k == 0), stop=(k == KC - 1))
                            mm.then_inc(proj, 1)

            def residual_bias(tb, q):
                residual(tb, q)
                pe.matmul(ps[:, Q * tb + q, :], ones[0:1, :], bias_row[0:1, q * 512:(q + 1) * 512],
                          start=False, stop=True, skip_group_check=True)

            pe.wait_ge(glu_done, 4 + KC)
            pe.wait_ge(bias_loaded, 16)
            for b in range(6):
                residual_bias(b // Q, b % Q)
            for k in range(KC):
                pe.wait_ge(conv_steps, (W + 1) * (k + 2))
                mm = pe.matmul(ps[:, 7, 0:S], mean_ones[:, :], conv[:, k, :], start=(k == 0), stop=(k == KC - 1))
            mm.then_inc(ch_stat, 1)
            for k in range(KC):
                pe.wait_ge(ch_act, k // 4 + 1)
                mm = pe.matmul(ps[:, 6, 0:S], mean_ones[:, :], squares[:, k, :], start=(k == 0), stop=(k == KC - 1))
            mm.then_inc(ch_stat, 1)
            pe.wait_ge(ch_steps, 5)
            residual_bias(1, 2)
            residual_bias(1, 3)
            project_tok(P_OUT, conv, lambda k: pe.wait_ge(ch_act, 6 + k))

            def peer(layer):
                turn_x(1 + 2 * layer)
                pe.wait_ge(sk_loaded, 16 * (layer + 1))
                for j in range(HC // 4):
                    pe.wait_ge(xt_taken, 8 * (1 + 2 * layer) + j + 1)
                    for c in range(4):
                        mm = pe.transpose(ps[:, j, c * P:(c + 1) * P], sk_raw[:, 4 * j + c, :], ident[:, :])
                    mm.then_inc(sk_ready, 1)
                pe.wait_ge(xt_taken, 8 * (2 + 2 * layer))
                pe.wait_ge(sk_taken, 4 * (layer + 1))
                with pe.Fori(0, PANELS // RING) as i:
                    for s in range(RING):
                        pe.wait_ge(panel[s], i * 16 + 16 * landed(P_WQ[layer] + s))
                        for m in range(2):
                            j = 2 * s + m
                            pe.wait_ge(score_taken, i * 8 + (HC * layer + j + 1))
                            for k in range(KC):
                                mm = pe.matmul(ps[:, j, 0:S], panel_chan(s)[:, k, m * P:(m + 1) * P], x_chan[:, k, :],
                                               start=(k == 0), stop=(k == KC - 1))
                            mm.then_inc(proj, 1)
                        for m in range(2):
                            j = 2 * s + m
                            pe.wait_ge(chunk_taken, i * 8 + (8 + 48 * layer + j + 1))
                            for tb in range(TB):
                                mm = pe.matmul(ps[:, j, S + tb * P:S + (tb + 1) * P], q_now[:, j, tb * P:(tb + 1) * P],
                                               sk_t[:, bass.ds(i * 8 + j, 1), :].rearrange("p a b -> p (a b)"),
                                               start=True, stop=True)
                            mm.then_inc(score_ready, 1)
                pe.wait_ge(score_taken, 8 + HC * (layer + 1))
                for tb in range(TB):
                    for q in range(Q):
                        residual(tb, q)
                    base = (layer * TB + tb) * GROUPS
                    with pe.Fori(0, GROUPS) as i:
                        for s in range(RING):
                            pe.wait_ge(diag_done, i * RING + (base * RING + s + 1))
                            pe.wait_ge(v_row[s], i * 16 + (base + 1) * 16)
                            for q in range(Q):
                                mm = pe.matmul(ps[:, Q * tb + q, :], diag[:, s, :], row_tile(1, s)[:, q * 512:(q + 1) * 512],
                                               start=False, stop=True, skip_group_check=True)
                            mm.then_inc(v_used, 1)

            peer(0)

            turn_x(2)
            pe.wait_ge(x_split, 8)
            split_chan(0, 16)
            pe.wait_ge(chunk_taken, 8 + 32)
            split_tok(HALVES)
            pe.wait_ge(v_taken, 8)
            split_chan(2 * HALVES, 32)
            pe.wait_ge(chunk_taken, 8 + 48)
            for it in range(HEADS + 2):
                if it < HEADS:
                    h = it
                    if h >= 2:
                        pe.wait_ge(z_copied, h - 1)
                        pe.wait_ge(z_soft, 2 * (h - 1))
                    pe.matmul(ps[:, h % 2, 0:S], k_t[:, h, 0:P], q_t[:, h, :], start=True, stop=True)
                    pe.matmul(ps[:, h % 2, S:AW], k_t[:, h, P:S], q_t[:, h, P:S], start=True, stop=True).then_inc(z_ready, 1)
                if 1 <= it <= HEADS:
                    h = it - 1
                    b = 2 + h % 2
                    pe.wait_ge(z_soft, 2 * (h + 1))
                    if h >= 2:
                        pe.wait_ge(z_logit, h - 1)
                    pe.matmul(ps[:, b, 0:S], tri[:, :], soft_b[:, h % 2, 0:S], start=True, stop=False, skip_group_check=True)
                    pe.matmul(ps[:, b, P:S], ones[:, :], soft_b[:, h % 2, S:AW], start=False, stop=True, skip_group_check=True)
                    pe.matmul(ps[:, b, S:AW], tri[:, :], soft_b[:, h % 2, S:AW], start=True, stop=True,
                              skip_group_check=True).then_inc(rest_ready, 1)
                if it >= 2:
                    h = it - 2
                    b = 4 + h % 2
                    pe.wait_ge(att_masked, h + 1)
                    if h >= 2:
                        pe.wait_ge(o_copied, h - 1)
                    pe.matmul(ps[:, b, 0:S], v_tok[:, 0, h * P:(h + 1) * P], att[:, h % 2, 0:S],
                              start=True, stop=False, skip_group_check=True)
                    pe.matmul(ps[:, b, P:S], v_tok[:, 1, h * P:(h + 1) * P], att[:, h % 2, S:AW],
                              start=False, stop=True, skip_group_check=True).then_inc(o_ready, 1)
            pe.wait_ge(o_copied, HEADS)
            for b in range(8):
                residual(b // Q, b % Q)
            project_tok(P_O, o_t, lambda k: None)
            peer(1)

        @block.scalar
        def _(act):
            act.sem_inc(chunk_taken, 8)
            act.sem_inc(score_taken, 8)

            def take_x(n):
                for b in range(8):
                    tb, j = b // Q, b % Q
                    act.wait_ge(xt_ready, 8 * n + b + 1)
                    to = x_hi if n == 2 else x_chan
                    act.activation(to[:, 4 * j:4 * j + 4, tb * P:(tb + 1) * P],
                                   ps[:, b, :].rearrange("p (a b) -> p a b", a=4), ACT.Copy).then_inc(xt_taken, 1)

            def norm(n, tb):
                v = lnv[:, tb, :]
                act.wait_ge(ln_steps[n], LN_STEPS * tb + 6)
                act.activation(v[:, 1:2], v[:, 0:1], ACT.Sqrt).then_inc(ln_act[n], 1)
                act.wait_ge(ln_steps[n], LN_STEPS * tb + 8)
                act.activation(x_tok[:, tb, :], bank_cols(tb), ACT.Identity, scale=v[:, 2:3], bias=v[:, 3:4]).then_inc(ln_act[n], 1)

            def gate_exp(layer, tb, half):
                act.wait_ge(route[layer], part_at(tb, half) + PART_LOGITS)
                part = logits[:, half * (PH // 2):(half + 1) * (PH // 2), :]
                act.activation(part, part, ACT.Exp).then_inc(route_exp, 1)

            act.wait_ge(vec_t, 1)
            act.activation(vec[:, :], ps[:, 0, 0:NB_IN + 3 * KC], ACT.Copy).then_inc(vec_taken, 1)
            act.wait_ge(vec_t, 2)
            act.activation(taps[:, :], ps[:, 1, 0:W * KC], ACT.Copy).then_inc(vec_taken, 1)
            take_x(0)
            act.wait_ge(vec_taken, 2)

            with act.Fori(0, KC // 4) as i:
                for b in range(4):
                    act.wait_ge(proj, i * 8 + (4 * (b // 2) + b % 2 + 3))
                    act.sem_inc(act_tick, 1)
                    act.wait_ge(glu_done, i * 4 + (b + 3))
                    act.sem_inc(act_tick, 1)
                    act.activation(sig[:, b % 2, :], ps[:, b, S:2 * S], ACT.Sigmoid,
                                   bias=vec[:, bass.ds(i * 4 + (KC + b), 1)]).then_inc(sig_ready, 1)

            for q in range(4):
                act.wait_ge(ch_steps, q + 1)
                act.activation(squares[:, 4 * q:4 * q + 4, :], conv[:, 4 * q:4 * q + 4, :], ACT.Square).then_inc(ch_act, 1)
            act.wait_ge(ch_steps, 5)
            act.activation(ch_rstd[:, 1, :], ch_rstd[:, 0, :], ACT.Sqrt).then_inc(ch_act, 1)
            for k in range(KC):
                act.wait_ge(ch_steps, 7 + k // 4)
                act.activation(conv[:, k, :], conv[:, k, :], ACT.Silu, scale=vec[:, NB_IN + KC + k:NB_IN + KC + k + 1],
                               bias=vec[:, NB_IN + 2 * KC + k:NB_IN + 2 * KC + k + 1]).then_inc(ch_act, 1)

            def peer(layer):
                for tb in range(TB):
                    norm(2 * layer, tb)
                take_x(1 + 2 * layer)
                for j in range(4):
                    act.wait_ge(sk_ready, 4 * layer + j + 1)
                    act.activation(sk_t[:, 4 * j:4 * j + 4, :], ps[:, j, :].rearrange("p (a b) -> p a b", a=4),
                                   ACT.Copy).then_inc(sk_taken, 1)
                for c in range(0, HC, 2):
                    for m in range(c, c + 2):
                        act.wait_ge(proj, 2 * P_WQ[layer] + m + 1)
                        if m >= 8:
                            act.wait_ge(score_ready, HC * layer + m - 7)
                        act.activation(q_now[:, m % 8, :], ps[:, m % 8, 0:S], ACT.Copy).then_inc(chunk_taken, 1)
                    for m in range(c, c + 2):
                        act.wait_ge(score_ready, HC * layer + m + 1)
                        act.activation(score[:, :, m * NKEY:(m + 1) * NKEY],
                                       ps[:, m % 8, S:2 * S].rearrange("p (t k) -> p t k", t=TB), ACT.Copy).then_inc(score_taken, 1)
                    if c == 2 * EARLY_HEADS:
                        gate_exp(layer, 0, 0)
                gate_exp(layer, 0, 1)
                for tb in range(TB):
                    for half in range(2):
                        base = (layer * TB + tb) * GROUPS + half * (GROUPS // 2)
                        with act.Fori(0, GROUPS // 2) as i:
                            act.wait_ge(u_used, i * RING + (base * RING + 2 * RING))
                            act.activation(gelu_now[:, :], h_now[:, :], ACT.Gelu).then_inc(gelu_done, 1)
                            act.wait_ge(coef_done, i + (base + 1))
                            for s in range(RING):
                                act.wait_ge(v_used, i * RING + (base * RING + s + 1))
                                act.activation(diag[:, s, :], ident[:, :], ACT.Copy, scale=coef_now[:, s:s + 1]).then_inc(diag_done, 1)
                        if tb == 0:
                            gate_exp(layer, 1, half)
                    norm(2 * layer + 1, tb)

            peer(0)
            take_x(2)
            for u in range(3 * HALVES + 2):
                if u < 3 * HALVES:
                    if u % 2 == 0:
                        act.wait_ge(panel[(u // 2) % 2], 16 * landed(P_K + u // 2))
                    act.wait_ge(proj, 2 * P_K + u - 1)
                    act.activation(half_as(w_hi, u), raw_half(u), ACT.Copy).then_inc(w_rounded, 1)
                c = u - 2
                if 0 <= c and not HALVES <= c < 2 * HALVES:
                    act.wait_ge(proj, 2 * P_K + c + 1)
                    act.activation((k_t if c < HALVES else q_t)[:, c % HALVES, :], ps[:, c % 8, 0:S], ACT.Copy,
                                   scale=1.0 if c < HALVES else SCALE).then_inc(chunk_taken, 1)
                elif c == 2 * HALVES - 1:
                    act.wait_ge(first_sum, 2)
                    for b in range(8):
                        if b == Q:
                            act.wait_ge(proj, 2 * P_Q)
                        act.activation(v_tok[:, b // Q, (b % Q) * 512:(b % Q + 1) * 512], ps[:, b, :], ACT.Copy).then_inc(v_taken, 1)
            act.preload_act_table_set("natural_log_exp_and_others")
            for it in range(HEADS + 2):
                if it < HEADS:
                    h = it
                    act.wait_ge(z_ready, h + 1)
                    if h >= 2:
                        act.wait_ge(z_logit, h - 1)
                    act.activation(zc[:, h % 2, :], ps[:, h % 2, 0:AW], ACT.Copy).then_inc(z_copied, 1)
                    act.wait_ge(z_abs, h + 1)
                    act.activation(soft_a[:, h % 2, :], soft_a[:, h % 2, :], ACT.Exp, scale=-1.0).then_inc(z_log, 1)
                    act.wait_ge(z_log, 2 * h + 1)
                    act.activation(soft_a[:, h % 2, :], soft_a[:, h % 2, :], ACT.Ln, bias=1.0).then_inc(z_log, 1)
                if 1 <= it <= HEADS:
                    h = it - 1
                    act.wait_ge(z_logit, h + 1)
                    if h >= 2:
                        act.wait_ge(o_ready, h - 1)
                    act.activation(att[:, h % 2, :], soft_a[:, h % 2, :], ACT.Exp).then_inc(att_exp, 1)
                if it >= 2:
                    h = it - 2
                    act.wait_ge(o_ready, h + 1)
                    act.activation(o_t[:, h, :], ps[:, 4 + h % 2, 0:S], ACT.Copy).then_inc(o_copied, 1)
            peer(1)

        @block.vector
        def _(dve):
            dve.sem_inc(u_used, RING)
            dve.sem_inc(glu_done, 4)

            dve.memset(hpad[:, :, 0:PAD], 0.0).then_inc(conv_steps, W + 1)
            dve.wait_ge(vec_taken, 2)
            taps_by = taps[:, :].rearrange("p (w c) -> p w c", c=KC)
            STEPS = W + 1
            with dve.Fori(0, KC // 4) as i:
                for b in range(4):
                    e = b % 2
                    at = (b + 1) * STEPS
                    dve.wait_ge(sig_ready, i * 4 + (b + 1))
                    dve.scalar_tensor_tensor(out=hpad[:, e, PAD:], in0=ps[:, b, 0:S], scalar=vec[:, bass.ds(i * 4 + b, 1)],
                                             in1=sig[:, e, :], op0=ALU.add, op1=ALU.mult).then_inc(glu_done, 1)
                    dve.tensor_copy(tap_c[:, e, :], taps_by[:, :, bass.ds(i * 4 + b, 1)].rearrange("p w c -> p (w c)")) \
                       .then_inc(conv_steps, 1)
                    dve.wait_ge(conv_steps, i * (4 * STEPS) + (at + 1))
                    dve.wait_ge(glu_done, i * 4 + (4 + b + 1))
                    dve.tensor_scalar(acc_c[:, e, :], hpad[:, e, 0:S], tap_c[:, e, 0:1],
                                      vec[:, bass.ds(i * 4 + (NB_IN + b), 1)], ALU.mult, ALU.add).then_inc(conv_steps, 1)
                    for w in range(1, W):
                        dve.wait_ge(conv_steps, i * (4 * STEPS) + (at + 1 + w))
                        to = acc_c[:, e, :] if w < W - 1 else conv[:, bass.ds(i * 4 + b, 1), :].rearrange("p a b -> p (a b)")
                        dve.scalar_tensor_tensor(out=to, in0=hpad[:, e, w:w + S], scalar=tap_c[:, e, w:w + 1],
                                                 in1=acc_c[:, e, :], op0=ALU.mult, op1=ALU.add).then_inc(conv_steps, 1)

            dve.wait_ge(ch_stat, 1)
            for q in range(4):
                c = conv[:, 4 * q:4 * q + 4, :]
                dve.tensor_tensor(out=c, in0=c, in1=ps[:, 7:8, 0:S].to_broadcast([P, 4, S]), op=ALU.subtract).then_inc(ch_steps, 1)
            dve.wait_ge(ch_stat, 2)
            dve.tensor_scalar(ch_rstd[:, 0, :], ps[:, 6, 0:S], LN_EPS, None, ALU.add).then_inc(ch_steps, 1)
            dve.wait_ge(ch_act, 5)
            dve.reciprocal(ch_rstd[:, 0, :], ch_rstd[:, 1, :]).then_inc(ch_steps, 1)
            dve.wait_ge(ch_steps, 6)
            for q in range(4):
                c = conv[:, 4 * q:4 * q + 4, :]
                dve.tensor_tensor(out=c, in0=c, in1=ch_rstd[:, 0:1, :].to_broadcast([P, 4, S]), op=ALU.mult).then_inc(ch_steps, 1)

            def norm(n, tb):
                at = LN_STEPS * tb
                for q in range(Q):
                    dve.bn_stats(stats[:, tb, q, :], ps[:, Q * tb + q, :]).then_inc(ln_steps[n], 1)
                dve.wait_ge(ln_steps[n], at + 4)
                dve.bn_aggr(mv[:, tb, :], stats[:, tb, :, :]).then_inc(ln_steps[n], 1)
                dve.wait_ge(ln_steps[n], at + 5)
                dve.tensor_scalar(lnv[:, tb, 0:1], mv[:, tb, 1:2], LN_EPS, None, ALU.add).then_inc(ln_steps[n], 1)
                dve.wait_ge(ln_act[n], 2 * tb + 1)
                dve.reciprocal(lnv[:, tb, 2:3], lnv[:, tb, 1:2]).then_inc(ln_steps[n], 1)
                dve.wait_ge(ln_steps[n], at + 7)
                dve.scalar_tensor_tensor(out=lnv[:, tb, 3:4], in0=mv[:, tb, 0:1], scalar=-1.0, in1=lnv[:, tb, 2:3],
                                         op0=ALU.mult, op1=ALU.mult).then_inc(ln_steps[n], 1)
                dve.wait_ge(ln_act[n], 2 * tb + 2)
                dve.wait_ge(rows_loaded, 32 * (n + 1))
                dve.tensor_tensor(out=x_tok[:, tb, :], in0=x_tok[:, tb, :], in1=ln_rows[:, 0, :], op=ALU.mult).then_inc(ln_steps[n], 1)
                dve.wait_ge(ln_steps[n], at + 9)
                dve.tensor_tensor(out=x_tok[:, tb, :], in0=x_tok[:, tb, :], in1=ln_rows[:, 1, :], op=ALU.add).then_inc(ln_steps[n], 1)

            def top16(values, indices, table, rows, at, done):
                for r in range(rows):
                    dve.max(values(r)[:, 0:8], table(r)).then_inc(done, 1)
                dve.wait_ge(done, at + rows)
                for r in range(rows):
                    dve.max_index(indices(r)[:, 0:8], values(r)[:, 0:8], table(r)).then_inc(done, 1)
                dve.wait_ge(done, at + 2 * rows)
                for r in range(rows):
                    dve.match_replace(table(r), values(r)[:, 0:8], table(r), -3.0e38).then_inc(done, 1)
                dve.wait_ge(done, at + 3 * rows)
                for r in range(rows):
                    dve.max(values(r)[:, 8:16], table(r)).then_inc(done, 1)
                dve.wait_ge(done, at + 4 * rows)
                for r in range(rows):
                    dve.max_index(indices(r)[:, 8:16], values(r)[:, 8:16], table(r)).then_inc(done, 1)
                dve.wait_ge(done, at + 5 * rows)

            def route_head(layer, h):
                done = route[layer]
                at = head_at(h)
                dve.wait_ge(score_taken, 8 + HC * layer + 2 * h + 2)
                top16(lambda r: key_s[:, r // 2, 2 * h + r % 2, :], lambda r: key_i[:, r // 2, 2 * h + r % 2, :],
                      lambda r: score[:, r // 2, (2 * h + r % 2) * NKEY:(2 * h + r % 2 + 1) * NKEY], 2 * TB, at, done)
                dve.tensor_tensor(out=pair_s[:, :, :].rearrange("p t (a b) -> p t a b", a=TOPK),
                                  in0=key_s[:, :, 2 * h, :].unsqueeze(3).to_broadcast([P, TB, TOPK, TOPK]),
                                  in1=key_s[:, :, 2 * h + 1, :].unsqueeze(2).to_broadcast([P, TB, TOPK, TOPK]),
                                  op=ALU.add).then_inc(done, 1)
                dve.wait_ge(done, at + 21)
                top16(lambda r: best_s[:, r, h, :], lambda r: best_j[:, r, h, :], lambda r: pair_s[:, r, :], TB, at + 21, done)

            def route_part(layer, tb, half):
                done = route[layer]
                at = part_at(tb, half)
                HH, HS = PH // 2, SLOTS // 2
                heads, slots = slice(half * HH, (half + 1) * HH), slice(half * HS, (half + 1) * HS)
                best = best_s[:, tb, heads, :]
                dve.tensor_tensor(out=logits[:, heads, :], in0=best, in1=best[:, :, 0:1].to_broadcast([P, HH, TOPK]),
                                  op=ALU.subtract).then_inc(done, 1)
                flat_j = best_j[:, tb, heads, :].rearrange("p h k -> p (h k)")
                dve.tensor_scalar(row_j[:, 0, slots], flat_j, 4, None, ALU.logical_shift_right).then_inc(done, 1)
                dve.tensor_scalar(row_j[:, 1, slots], flat_j, TOPK - 1, None, ALU.bitwise_and).then_inc(done, 1)
                dve.wait_ge(done, at + 3)
                dve.tensor_copy(row_f[:, 0, slots], row_j[:, 0, slots]).then_inc(done, 1)
                dve.tensor_copy(row_f[:, 1, slots], row_j[:, 1, slots]).then_inc(done, 1)
                key_rows = slice(half * (HC // 2), (half + 1) * (HC // 2))
                dve.tensor_copy(key_f[:, key_rows, :], key_i[:, tb, key_rows, :]).then_inc(done, 1)
                dve.wait_ge(done, at + 6)
                keys = key_f[:, key_rows, :].rearrange("p (h c) k -> p h c k", c=2)
                hot_s = hot[:, slots, :]
                hot_hk = hot_s.rearrange("p (h k) a -> p h k a", h=HH)
                for c in range(2):
                    dve.tensor_tensor(out=hot_s, in0=row_f[:, c, slots].unsqueeze(2).to_broadcast([P, HS, TOPK]),
                                      in1=iota_f[:, :].unsqueeze(1).to_broadcast([P, HS, TOPK]), op=ALU.is_equal).then_inc(done, 1)
                    dve.wait_ge(done, at + 7 + 3 * c)
                    dve.tensor_tensor(out=hot_hk, in0=hot_hk, in1=keys[:, :, c, :].unsqueeze(2).to_broadcast([P, HH, TOPK, TOPK]),
                                      op=ALU.mult).then_inc(done, 1)
                    dve.wait_ge(done, at + 8 + 3 * c)
                    dve.tensor_reduce(row_e[:, c, slots], hot_s, AX_X, ALU.add).then_inc(done, 1)
                    dve.wait_ge(done, at + 9 + 3 * c)
                dve.scalar_tensor_tensor(out=row_e[:, 0, slots], in0=row_e[:, 0, slots], scalar=float(NKEY), in1=row_e[:, 1, slots],
                                         op0=ALU.mult, op1=ALU.add).then_inc(done, 1)
                dve.wait_ge(done, at + 13)
                dve.tensor_scalar(index[:, tb, slots], row_e[:, 0, slots], float(layer * NEXP), None, ALU.add).then_inc(done, 1)
                dve.wait_ge(route_exp, 2 * TB * layer + 2 * tb + half + 1)
                dve.tensor_reduce(gsum[:, 0, heads], logits[:, heads, :], AX_X, ALU.add).then_inc(done, 1)
                dve.wait_ge(done, at + 15)
                dve.reciprocal(gsum[:, 1, heads], gsum[:, 0, heads]).then_inc(done, 1)
                dve.wait_ge(done, at + 16)
                dve.tensor_tensor(out=gate[:, tb, slots].rearrange("p (h k) -> p h k", k=TOPK), in0=logits[:, heads, :],
                                  in1=gsum[:, 1, heads].unsqueeze(2).to_broadcast([P, HH, TOPK]), op=ALU.mult).then_inc(done, 1)
                dve.wait_ge(done, at + 17)

            def peer(layer):
                dve.wait_ge(first_sum, 2 * layer + 1)
                norm(2 * layer, 0)
                dve.wait_ge(proj, 2 * (P_WQ[layer]))
                norm(2 * layer, 1)
                for h in range(PH):
                    if h == EARLY_HEADS:
                        route_part(layer, 0, 0)
                    route_head(layer, h)
                route_part(layer, 0, 1)
                for tb in range(TB):
                    for half in range(2):
                        base = (layer * TB + tb) * GROUPS + half * (GROUPS // 2)
                        with dve.Fori(0, GROUPS // 2) as i:
                            for s in range(RING):
                                dve.wait_ge(u_row[s], i * 16 + (base + 1) * 16)
                                dve.scalar_tensor_tensor(out=row_tile(0, s), in0=row_tile(0, s), scalar=1.0, in1=x_tok[:, tb, :],
                                                         op0=ALU.mult, op1=ALU.mult, accum_out=h_now[:, s:s + 1]).then_inc(u_used, 1)
                            if layer or tb or half:
                                dve.wait_ge(diag_done, i * RING + base * RING)
                            dve.wait_ge(gelu_done, i + (base + 1))
                            dve.tensor_tensor(out=coef_now[:, :], in0=gelu_now[:, :],
                                              in1=gate[:, tb, bass.ds(i * RING + half * (SLOTS // 2), RING)],
                                              op=ALU.mult).then_inc(coef_done, 1)
                        if tb == 0:
                            route_part(layer, 1, half)
                    dve.wait_ge(v_used, RING + (layer * TB + tb + 1) * SLOTS)
                    norm(2 * layer + 1, tb)

            peer(0)

            for b in range(8):
                tb, j = b // Q, b % Q
                dve.wait_ge(xt_taken, 16 + b + 1)
                part = (slice(None), slice(4 * j, 4 * j + 4), slice(tb * P, (tb + 1) * P))
                dve.tensor_tensor(out=x_lo[part], in0=ps[:, b, :].rearrange("p (a b) -> p a b", a=4),
                                  in1=x_hi[part].bitcast(F32), op=ALU.subtract).then_inc(x_split, 1)
            for u in range(3 * HALVES):
                dve.wait_ge(w_rounded, u + 1)
                dve.wait_ge(proj, 2 * P_K + u - 1)
                dve.tensor_tensor(out=half_as(w_lo, u), in0=raw_half(u), in1=half_as(w_hi, u).bitcast(F32),
                                  op=ALU.subtract).then_inc(w_split, 1)

            for it in range(HEADS + 1):
                if it < HEADS:
                    h = it
                    e = h % 2
                    z = ps[:, e, 0:AW]
                    dve.wait_ge(z_copied, h + 1)
                    if h >= 2:
                        dve.wait_ge(att_exp, h - 1)
                    dve.scalar_tensor_tensor(out=soft_a[:, e, :], in0=z, scalar=-1.0, in1=zc[:, e, :],
                                             op0=ALU.mult, op1=ALU.max).then_inc(z_abs, 1)
                    dve.wait_ge(z_log, 2 * h + 2)
                    if h >= 2:
                        dve.wait_ge(rest_ready, h - 1)
                    dve.scalar_tensor_tensor(out=soft_b[:, e, :], in0=z, scalar=0.0, in1=soft_a[:, e, :],
                                             op0=ALU.max, op1=ALU.add).then_inc(z_soft, 1)
                    dve.wait_ge(z_soft, 2 * h + 1)
                    diagonal = soft_b[:, e, :].rearrange("p (a b) -> p a b", b=P)[:, 0:3:2, :]
                    dve.tensor_tensor(out=diagonal, in0=diagonal, in1=causal[:, :].unsqueeze(1).to_broadcast([P, 2, P]),
                                      op=ALU.mult).then_inc(z_soft, 1)
                if it >= 1:
                    h = it - 1
                    e = h % 2
                    dve.wait_ge(rest_ready, h + 1)
                    dve.wait_ge(z_copied, h + 1)
                    dve.tensor_tensor(out=soft_a[:, e, :], in0=zc[:, e, :], in1=ps[:, 2 + e, 0:AW], op=ALU.subtract).then_inc(z_logit, 1)
                    dve.wait_ge(att_exp, h + 1)
                    diagonal = att[:, e, :].rearrange("p (a b) -> p a b", b=P)[:, 0:3:2, :]
                    dve.scalar_tensor_tensor(out=diagonal, in0=diagonal, scalar=1.0,
                                             in1=causal[:, :].unsqueeze(1).to_broadcast([P, 2, P]),
                                             op0=ALU.min, op1=ALU.mult).then_inc(att_masked, 1)
            peer(1)


_INS = ["x", "conv_w_in", "conv_b_in", "conv_w_dw", "conv_b_dw", "conv_ln_g", "conv_ln_b", "conv_w_out", "conv_b_out",
        "attn_w_kv", "attn_w_q", "attn_w_o", "peer_w_q", "peer_sub_keys", "peer_u", "peer_v", "ln_g", "ln_b"]


def kernel(**inputs):
    import numpy as np
    import concourse.bacc as bacc
    from concourse.bass_utils import run_bass_kernel_spmd

    nc = bacc.Bacc("TRN2", target_bir_lowering=False, num_devices=1)
    arrays, args = {}, []
    for name in _INS:
        a = np.ascontiguousarray(inputs[name])
        arrays[f"in_{name}"] = a
        args.append(nc.dram_tensor(f"in_{name}", a.shape, mybir.dt.from_np(a.dtype), kind="ExternalInput").ap())
    out = nc.dram_tensor("out_dram", inputs["x"].shape, F32, kind="ExternalOutput").ap()
    build(nc, *args, out)
    r = run_bass_kernel_spmd(nc, [arrays], core_ids=[0])
    return r.results[0]["out_dram"]
```

```python
from contextlib import ExitStack

import concourse.bass as bass
from concourse import mybir

F32 = mybir.dt.float32
F32R = mybir.dt.float32r
U32 = mybir.dt.uint32
ALU = mybir.AluOpType
ACT = mybir.ActivationFunctionType
AX_X = mybir.AxisListType.X

P = 128
LN_EPS = 1e-5
TOPK = 16
RING = 4
LN_STEPS = 12
LN_HEAD = 8
HEAD_STEPS = 31
PART_LOGITS = 1
PART_INDEX = 14
PART_STEPS = 17
PILOT = 4
CONV_ORDER = (0, 1, 2, 3, 4, 5, 6, 7, 9, 10, 11, 8, 13, 14, 12, 15)
CH_DIVIDED = (7, 9, 11, 13)
EARLY_HEADS = 5


def build(nc, x, conv_w_in, conv_b_in, conv_w_dw, conv_b_dw, conv_ln_g, conv_ln_b, conv_w_out, conv_b_out,
          attn_w_kv, attn_w_q, attn_w_o, peer_w_q, peer_sub_keys, peer_u, peer_v, ln_g, ln_b, out):
    _, S, D = x.shape
    KC = D // P
    TB = S // P
    W = conv_w_dw.shape[1]
    PAD = W - 1
    HEADS = D // P
    LAYERS, PH, _, NKEY, DQ = peer_sub_keys.shape
    HC = PH * 2
    NEXP = peer_u.shape[1]
    SLOTS = PH * TOPK
    GROUPS = SLOTS // RING
    ALPHA = (2.0 * LAYERS) ** 0.25
    SCALE = float(P) ** -0.5

    def head_at(h):
        return HEAD_STEPS * h + (PART_STEPS if h >= EARLY_HEADS else 0)

    def part_at(tb, half):
        n = 2 * tb + half
        return HEAD_STEPS * (PH if n else EARLY_HEADS) + PART_STEPS * n
    Q = D // 512
    PANELS = 8
    assert TB == 2 and KC == 16 and Q == 4 and NKEY == P and DQ == P and HC == KC

    P_OUT, P_WQ = 2 * PANELS, [3 * PANELS, 8 * PANELS]
    P_K, P_V, P_Q, P_O = 4 * PANELS, 5 * PANELS, 6 * PANELS, 7 * PANELS
    HALVES = 2 * PANELS

    def first_half(n):
        return 2 * (n - P_OUT)

    IN_HALVES = 2 * P_OUT
    U_OUT, U_WQ = first_half(P_OUT), [first_half(n) for n in P_WQ]
    U_K, U_V, U_Q, U_O = first_half(P_K), first_half(P_V), first_half(P_Q), first_half(P_O)
    TOKEN_MAJOR = (range(U_OUT, U_OUT + HALVES), range(U_V, U_V + HALVES), range(U_O, U_O + HALVES))

    with ExitStack() as ctx:
        def sb(name, shape, dt=F32):
            return ctx.enter_context(nc.sbuf_tensor(name, shape, dt))

        def sem(name):
            return ctx.enter_context(nc.semaphore(name))

        ps = ctx.enter_context(nc.psum_tensor("ps", [P, 8, 512], F32))
        x_tok = sb("x_tok", [P, TB, D])
        x_chan_at = nc.sbuf_base
        x_chan = sb("x_chan", [P, KC, S])
        ring_at = nc.sbuf_base
        ring = sb("ring", [P, RING, 2 * D])
        ln_rows = sb("ln_rows", [P, 2, D])
        ident = sb("ident", [P, P])
        alpha_ident = sb("alpha_ident", [P, P])
        ones = sb("ones", [P, P])
        mean_ones = sb("mean_ones", [P, P])
        pilot_ones = sb("pilot_ones", [P, P])
        tri = sb("tri", [P, P])
        causal = sb("causal", [P, P])
        iota_i = sb("iota_i", [P, TOPK], mybir.dt.int32)
        iota_f = sb("iota_f", [P, TOPK])
        NB_IN = 2 * KC
        vec = sb("vec", [P, NB_IN + 3 * KC])
        taps = sb("taps", [P, W * KC])
        stats = sb("stats", [P, TB, Q, 6])
        mv = sb("mv", [P, TB, 2])
        lnv = sb("lnv", [P, TB, 3])
        index = sb("index", [P, TB, SLOTS], U32)
        gate = sb("gate", [P, TB, SLOTS])
        index_now = sb("index_now", [P, 2, RING], U32)
        h_now = sb("h_now", [P, RING])
        gelu_now = sb("gelu_now", [P, RING])
        coef_now = sb("coef_now", [P, RING])
        diag = sb("diag", [P, RING, P])
        logits = sb("logits", [P, PH, TOPK])
        row_j = sb("row_j", [P, 2, SLOTS], U32)
        row_f = sb("row_f", [P, 2, SLOTS])
        row_e = sb("row_e", [P, 2, SLOTS])
        gsum = sb("gsum", [P, 2, PH])
        work_at = nc.sbuf_base
        work = sb("work", [P, 19500])
        x_hi = nc.alloc_sbuf_tensor_at("x_hi", [P, KC, S], F32R, offset=x_chan_at)
        x_lo = nc.alloc_sbuf_tensor_at("x_lo", [P, KC, S], F32R, offset=work_at + 4 * 12288)
        conv_lo = nc.alloc_sbuf_tensor_at("conv_lo", [P, KC, S], F32R, offset=work_at + 4 * 4096)
        o_hi = nc.alloc_sbuf_tensor_at("o_hi", [P, KC, S], F32R, offset=work_at)
        o_lo = nc.alloc_sbuf_tensor_at("o_lo", [P, KC, S], F32R, offset=work_at + 4 * 8192)
        w_hi = nc.alloc_sbuf_tensor_at("w_hi", [P, 2, D], F32R, offset=ring_at + 4 * 2 * 2 * D)
        w_lo = nc.alloc_sbuf_tensor_at("w_lo", [P, 2, D], F32R, offset=ring_at + 4 * 3 * 2 * D)

        def view(at, *shape):
            n = 1
            for d in shape:
                n *= d
            v = work[:, at:at + n]
            if len(shape) == 2:
                return v.rearrange("p (a b) -> p a b", a=shape[0])
            if len(shape) == 3:
                return v.rearrange("p (a b c) -> p a b c", a=shape[0], b=shape[1])
            return v

        conv = view(0, KC, S)
        squares = view(4096, KC, S)
        sig = view(8192, 2, S)
        hpad = view(8704, 2, PAD + S)
        acc_c = view(9300, 2, S)
        tap_c = view(9820, 2, W)
        ch_rstd = view(9900, 2, S)
        pilot = view(12288 + 1200, S)
        ch_mean = view(12288 + 1500, S)
        ch_msq = view(12288 + 1800, S)
        pool_pad = view(14400, PAD + S)
        pool_sum = view(14700, S)
        pool_prod = view(14960, 3, S)
        pool_tap = view(15740, W + 1)
        vec_raw = view(10500, P)
        taps_raw = view(10700, 4, P)
        bias_row = view(11300, D)
        q_now = view(0, 8, S)
        key_s = view(2048, TB, HC, TOPK)
        key_i = view(2560, TB, HC, TOPK).bitcast(U32)
        key_f = view(3072, HC, TOPK)
        best_s = view(3328, TB, PH, TOPK)
        best_j = view(3584, TB, PH, TOPK).bitcast(U32)
        score = view(4096, TB, HC * NKEY)
        pair_s = view(8192, TB, TOPK * TOPK)
        hot = view(16384, SLOTS, TOPK)
        sk_raw = view(16384, HC, P)
        sk_t = view(8704, HC, P)
        k_t = view(0, HEADS, S)
        v_tok = view(4096, TB, D)
        q_t = view(8192, HEADS, S)
        AW = S + P
        att = view(16384, 5, AW)
        soft = view(16384 + 5 * AW, 3, AW)

        consts = sem("consts")
        x_loaded, vec_loaded, bias_loaded = sem("x_loaded"), sem("vec_loaded"), sem("bias_loaded")
        rows_loaded, sk_loaded, stored = sem("rows_loaded"), sem("sk_loaded"), sem("stored")
        panel = [sem(f"panel{i}") for i in range(RING)]
        u_row = [sem(f"u_row{i}") for i in range(RING)]
        v_row = [sem(f"v_row{i}") for i in range(RING)]
        vec_t, vec_taken = sem("vec_t"), sem("vec_taken")
        xt_ready, xt_taken = sem("xt_ready"), sem("xt_taken")
        first_sum = sem("first_sum")
        bank_sum = sem("bank_sum")
        x_split = sem("x_split")
        conv_split, o_split = sem("conv_split"), sem("o_split")
        w_rounded, w_split = sem("w_rounded"), sem("w_split")
        proj = sem("proj")
        chunk_taken = sem("chunk_taken")
        sig_ready = sem("sig_ready")
        glu_done = sem("glu_done")
        conv_steps = sem("conv_steps")
        ch_stat, ch_steps, ch_act = sem("ch_stat"), sem("ch_steps"), sem("ch_act")
        pool_free = sem("pool_free")
        pool_fed = sem("pool_fed")
        pool_steps = sem("pool_steps")
        shifted, squared = sem("shifted"), sem("squared")
        ln_steps = [sem(f"ln_steps{i}") for i in range(4)]
        ln_act = [sem(f"ln_act{i}") for i in range(4)]
        sk_ready, sk_taken = sem("sk_ready"), sem("sk_taken")
        score_ready = sem("score_ready")
        score_taken = sem("score_taken")
        route = [sem(f"route{i}") for i in range(LAYERS)]
        route_exp = sem("route_exp")
        index_copied, pool_tick = sem("index_copied"), sem("pool_tick")
        u_used = sem("u_used")
        v_used = sem("v_used")
        gelu_done, coef_done, diag_done = sem("gelu_done"), sem("coef_done"), sem("diag_done")
        act_tick = sem("act_tick")
        v_taken = sem("v_taken")
        z_ready, rest_ready, o_ready = sem("z_ready"), sem("rest_ready"), sem("o_ready")
        z_abs, z_soft, z_logit, att_masked = sem("z_abs"), sem("z_soft"), sem("z_logit"), sem("att_masked")
        z_copied, z_log, att_exp, o_copied = sem("z_copied"), sem("z_log"), sem("att_exp"), sem("o_copied")

        u_tab = peer_u.rearrange("l e d -> (l e) d")
        v_tab = peer_v.rearrange("l e d -> (l e) d")

        def panel_chan(slot):
            return ring[:, slot, :].rearrange("p (c n) -> p c n", c=KC)

        def panel_tok(slot):
            return ring[:, slot, :].rearrange("p (c n) -> p c n", c=2)

        def landed(n):
            if n < P_OUT:
                return n // RING + 1
            return P_OUT // RING + (n - P_OUT) // 2 + 1

        def raw_half(u):
            slot, m = (u // 2) % 2, u % 2
            if any(u in r for r in TOKEN_MAJOR):
                return panel_tok(slot)[:, m, :]
            return panel_chan(slot)[:, :, m * P:(m + 1) * P]

        def half_as(buf, u):
            v = buf[:, u % 2, :]
            return v if any(u in r for r in TOKEN_MAJOR) else v.rearrange("p (c n) -> p c n", c=KC)

        def buffer_free(u):
            return max(IN_HALVES, IN_HALVES + u - 1)

        def row_tile(kind, i):
            return ring[:, 2 * kind + i // 2, (i % 2) * D:(i % 2 + 1) * D]

        def bank_cols(tb):
            return ps[:, Q * tb:Q * tb + Q, :].rearrange("p a b -> p (a b)")

        def wait_shifted(eng, k):
            if k < KC // 2:
                eng.wait_ge(shifted, k + 1)
            elif k % 4 == 0:
                eng.wait_ge(pool_free, 1 + k // 4 + 1)
            else:
                eng.wait_ge(shifted, KC // 2 + (3 * (k // 4 - 2) + k % 4))

        block = ctx.enter_context(nc.Block())

        @block.sync
        def _(sp):
            for tb in range(TB):
                sp.dma_start(x_tok[:, tb, :], x[0, tb * P:(tb + 1) * P, :]).then_inc(x_loaded, 16)

            def by_columns(w):
                return w.rearrange("(c p) n -> p c n", p=P)

            def load_chan(w, n, col):
                sp.dma_start(panel_chan(n % RING), by_columns(w)[:, :, col:col + 256]).then_inc(panel[n % RING], 16)

            def load_rows(n):
                if n:
                    sp.wait_ge(ln_steps[n - 1], TB * LN_STEPS)
                for i, w in enumerate((ln_g, ln_b)):
                    sp.dma_start(ln_rows[:, i, :], w[n // 2, n % 2:n % 2 + 1, :].partition_broadcast(P)) \
                      .then_inc(rows_loaded, 16)

            def load_keys(layer):
                sp.dma_start(sk_raw, peer_sub_keys[layer].rearrange("h c k d -> k (h c) d")).then_inc(sk_loaded, 16)

            sp.dma_start(vec_raw[0:NB_IN, :], conv_b_in.rearrange("l (r p) -> (l r) p", p=P)).then_inc(vec_loaded, 16)
            for i, w in enumerate((conv_b_dw, conv_ln_g, conv_ln_b)):
                at = NB_IN + i * KC
                sp.dma_start(vec_raw[at:at + KC, :], w.rearrange("l (r p) -> (l r) p", p=P)).then_inc(vec_loaded, 16)
            taps_by_row = conv_w_dw.rearrange("l w o (c p) -> (l w o c) p", p=P)
            RT = W * KC // 4
            sp.dma_start(taps_raw[0:RT, :, :], taps_by_row.rearrange("(r q) p -> q r p", q=RT)).then_inc(vec_loaded, 16)

            w_in = conv_w_in[0]
            for n in range(RING):
                load_chan(w_in, n, (n % 2) * D + (n // 2) * 256)
            load_rows(0)
            sp.dma_start(bias_row[0:1, :], conv_b_out).then_inc(bias_loaded, 16)
            load_keys(0)
            with sp.Fori(1, 2 * PANELS // RING) as i:
                for s in range(RING):
                    sp.wait_ge(proj, 2 * RING * i + (2 * s - 2 * RING + (2 if s % 2 else 3)))
                    sp.dma_start(panel_chan(s), by_columns(w_in)[:, :, bass.ds(i * 512 + ((s % 2) * D + (s // 2) * 256), 256)]) \
                      .then_inc(panel[s], 16)

            def load_split(w, n, p, token_major=False, col=0):
                local = n - P_OUT
                if local < 2:
                    sp.wait_ge(proj, IN_HALVES - 5 + local)
                elif n >= P_K + 2 or n < P_K:
                    sp.wait_ge(w_split, 2 * (local - 1))
                if token_major:
                    to, src = panel_tok(local % 2), by_columns(w)[:, 2 * p:2 * p + 2, col:col + D]
                else:
                    to, src = panel_chan(local % 2), by_columns(w)[:, :, p * 256:p * 256 + 256]
                sp.dma_start(to, src).then_inc(panel[local % 2], 16)

            for p in range(PANELS):
                load_split(conv_w_out[0], P_OUT + p, p, True)
            for p in range(PANELS):
                load_split(peer_w_q[0], P_WQ[0] + p, p)
            load_rows(1)
            sp.wait_ge(u_used, RING + TB * SLOTS)
            for p in range(PANELS):
                load_split(attn_w_kv, P_K + p, p)
            load_rows(2)
            for p in range(PANELS):
                load_split(attn_w_kv, P_V + p, p, True, D)
            for p in range(PANELS):
                load_split(attn_w_q[0], P_Q + p, p)
            for p in range(PANELS):
                load_split(attn_w_o[0], P_O + p, p, True)
                if p == 2:
                    sp.wait_ge(o_split, HEADS)
                    load_keys(1)
            for p in range(PANELS):
                load_split(peer_w_q[1], P_WQ[1] + p, p)
            load_rows(3)
            for tb in range(TB):
                for half in range(2):
                    sp.wait_ge(ln_steps[3], LN_STEPS * tb + LN_HEAD + 2 * half + 2)
                    cols = slice(half * (D // 2), (half + 1) * (D // 2))
                    sp.dma_start(out[0, tb * P:(tb + 1) * P, cols], x_tok[:, tb, cols]).then_inc(stored, 16)
            sp.wait_ge(stored, 16 * TB * 2)

        @block.gpsimd
        def _(pool):
            pool.memset(ones[:, :], 1.0).then_inc(consts, 1)
            pool.memset(mean_ones[:, :], 1.0 / D).then_inc(consts, 1)
            pool.memset(pilot_ones[:, :], 1.0 / (PILOT * P)).then_inc(consts, 1)
            pool.iota(iota_i[:, :], pattern=[[1, TOPK]], base=0, channel_multiplier=0).then_inc(consts, 1)
            pool.wait_ge(consts, 4)
            pool.affine_select(ident[:, :], ones[:, :], pattern=[[-1, P]], base=0, channel_multiplier=1,
                               compare_op=ALU.is_equal, fill=0.0).then_inc(consts, 1)
            pool.affine_select(tri[:, :], ones[:, :], pattern=[[-1, P]], base=0, channel_multiplier=1,
                               compare_op=ALU.is_ge, fill=0.0).then_inc(consts, 1)
            pool.affine_select(causal[:, :], ones[:, :], pattern=[[1, P]], base=0, channel_multiplier=-1,
                               compare_op=ALU.is_gt, fill=0.0).then_inc(consts, 1)
            pool.tensor_copy(iota_f[:, :], iota_i[:, :]).then_inc(consts, 1)
            pool.wait_ge(consts, 8)
            pool.tensor_scalar(alpha_ident[:, :], ident[:, :], ALPHA, None, ALU.mult).then_inc(consts, 1)

            STEPS = 2 * W - 1
            pool.sem_inc(pool_free, 1)
            pool.memset(pool_pad[:, 0:PAD], 0.0).then_inc(pool_steps, STEPS)

            def product(w):
                return pool.tensor_scalar(pool_prod[:, w % 3, :], pool_pad[:, w:w + S], pool_tap[:, w:w + 1], None, ALU.mult)

            def convolve(first, last):
                with pool.Fori(first, last) as i:
                    pool.wait_ge(glu_done, i * 4 + 5)
                    pool.sem_inc(pool_tick, 1)
                    pool.wait_ge(pool_fed, i * 2 + 2)
                    pool.sem_inc(pool_tick, 1)
                    pool.wait_ge(pool_steps, i * STEPS + STEPS)
                    pool.sem_inc(pool_tick, 1)
                    pool.tensor_scalar(pool_sum, pool_pad[:, 0:S], pool_tap[:, 0:1], pool_tap[:, W:W + 1],
                                       ALU.mult, ALU.add).then_inc(pool_steps, 1)
                    product(1).then_inc(pool_steps, 1)
                    for w in range(1, W):
                        if w + 1 < W:
                            product(w + 1).then_inc(pool_steps, 1)
                        pool.wait_ge(pool_steps, i * STEPS + (STEPS + 2 * w))
                        pool.tensor_tensor(out=pool_sum, in0=pool_sum, in1=pool_prod[:, w % 3, :], op=ALU.add).then_inc(pool_steps, 1)
                    pool.wait_ge(pool_steps, i * STEPS + 2 * STEPS)
                    pool.sem_inc(pool_tick, 1)
                    chunk = conv[:, bass.ds(i * 4, 1), :].rearrange("p a b -> p (a b)")
                    if first:
                        pool.tensor_tensor(out=chunk, in0=pool_sum, in1=pilot, op=ALU.subtract).then_inc(pool_free, 1)
                    else:
                        pool.tensor_copy(chunk, pool_sum).then_inc(pool_free, 1)

            convolve(0, 2)
            pool.wait_ge(ch_steps, 1)
            convolve(2, 4)

            def split_half(u):
                pool.wait_ge(w_rounded, u + 1)
                pool.wait_ge(proj, buffer_free(u))
                pool.tensor_tensor(out=half_as(w_lo, u), in0=raw_half(u), in1=half_as(w_hi, u).bitcast(F32),
                                   op=ALU.subtract).then_inc(w_split, 1)

            for u in range(2):
                split_half(U_OUT + u)

            for layer in range(LAYERS):
                pool.wait_ge(w_split, U_WQ[layer])
                for u in range(HALVES):
                    split_half(U_WQ[layer] + u)
                for tb in range(TB):
                    if tb == 0:
                        pool.wait_ge(w_split, U_WQ[layer] + HALVES)
                    for part in range(2):
                        pool.wait_ge(route[layer], part_at(tb, part) + PART_INDEX)
                        base = (layer * TB + tb) * GROUPS + part * (GROUPS // 2)
                        with pool.Fori(0, GROUPS // 4) as i:
                            for half in range(2):
                                pool.tensor_copy(index_now[:, half, :],
                                                 index[:, tb, bass.ds(i * (2 * RING) + (part * (SLOTS // 2) + half * RING), RING)]) \
                                    .then_inc(index_copied, 1)
                                pool.wait_ge(index_copied, i * 2 + (base + half + 1))
                                pool.sem_inc(pool_tick, 1)
                                pool.wait_ge(u_used, i * (2 * RING) + ((base + half) * RING + RING))
                                pool.sem_inc(pool_tick, 1)
                                for s in range(RING):
                                    pool.indirect_dma_start(
                                        row_tile(0, s), None, u_tab,
                                        bass.IndirectOffsetOnAxis(ap=index_now[:, half, s:s + 1], axis=0)).then_inc(u_row[s], 16)
                                if tb == 0 and part == 0 and half == 0:
                                    pool.wait_ge(proj, 2 * (P_WQ[layer] + PANELS))
                                pool.wait_ge(v_used, i * (2 * RING) + ((base + half) * RING + RING))
                                pool.sem_inc(pool_tick, 1)
                                for s in range(RING):
                                    pool.indirect_dma_start(
                                        row_tile(1, s), None, v_tab,
                                        bass.IndirectOffsetOnAxis(ap=index_now[:, half, s:s + 1], axis=0)).then_inc(v_row[s], 16)

        @block.tensor
        def _(pe):
            pe.sem_inc(v_used, RING)

            def turn_x(n):
                for tb in range(TB):
                    if n == 0 and tb == 0:
                        pe.wait_ge(x_loaded, 16 * TB)
                    for j in range(KC // 4):
                        if n:
                            pe.wait_ge(ln_steps[n - 1], LN_STEPS * tb + LN_HEAD + j + 1)
                        for c in range(4):
                            mm = pe.transpose(ps[:, Q * tb + j, c * P:(c + 1) * P],
                                              x_tok[:, tb, (4 * j + c) * P:(4 * j + c + 1) * P], ident[:, :])
                        mm.then_inc(xt_ready, 1)

            def passes(k, u, hi, lo, cols, x_cols):
                for w, xx in ((w_hi, hi), (w_hi, lo), (w_lo, hi)):
                    yield half_as(w, u)[:, k, cols] if cols is not None else half_as(w, u), xx[:, k, x_cols]

            def multiply_chan(u, j):
                for k in range(KC):
                    for t, (w, xx) in enumerate(passes(k, u, x_hi, x_lo, slice(0, P), slice(0, S))):
                        mm = pe.matmul(ps[:, j, 0:S], w, xx, start=(k == 0 and t == 0), stop=(k == KC - 1 and t == 2))
                mm.then_inc(proj, 1)

            def split_chan(u0, taken0):
                with pe.Fori(0, HALVES // 8) as i:
                    for j in range(8):
                        pe.wait_ge(w_split, i * 8 + (u0 + j + 1))
                        pe.wait_ge(chunk_taken, i * 8 + (taken0 + j + 1))
                        multiply_chan(u0 + j, j)

            def split_tok(u0, hi, lo, ready, add):
                def multiply(k, tb):
                    for q in range(Q):
                        if k == KC - 1 and q:
                            mm.then_inc(bank_sum, 1)
                        for t, (w, xx) in enumerate(passes(k, u0 + k, hi, lo, None, slice(tb * P, (tb + 1) * P))):
                            mm = pe.matmul(ps[:, Q * tb + q, :], xx, w[:, q * 512:(q + 1) * 512],
                                           start=(not add and k == 0 and t == 0), stop=(k == KC - 1 and t == 2),
                                           skip_group_check=True)
                    return mm

                for k in range(KC):
                    pe.wait_ge(w_split, u0 + k + 1)
                    ready(k)
                    mm = multiply(k, 0)
                    if k < KC - 2:
                        multiply(k, 1).then_inc(proj, 1)
                mm.then_inc(first_sum, 1)
                for k in range(KC - 2, KC):
                    multiply(k, 1).then_inc(proj, 1)

            def residual(tb, q):
                return pe.matmul(ps[:, Q * tb + q, :], alpha_ident[:, :], x_tok[:, tb, q * 512:(q + 1) * 512],
                                 start=True, stop=True, skip_group_check=True)

            pe.wait_ge(consts, 9)
            turn_x(0)
            pe.wait_ge(vec_loaded, 16 * 5)
            nv = NB_IN + 3 * KC
            pe.wait_ge(xt_taken, KC // 4 * TB)
            pe.transpose(ps[:, 6, 0:nv], vec_raw[0:nv, :], ident[0:nv, 0:nv]).then_inc(vec_t, 1)
            RT = W * KC // 4
            for r in range(4):
                mm = pe.transpose(ps[:, 7, r * RT:(r + 1) * RT], taps_raw[0:RT, r, :], ident[0:RT, 0:RT])
            mm.then_inc(vec_t, 1)

            def hidden(first, last):
                with pe.Fori(first, last) as i:
                    for pair in range(2):
                        for m in range(2):
                            bank = 2 * pair + m
                            pe.wait_ge(glu_done, i * 4 + (bank + 1))
                            for kind in range(2):
                                s = 2 * pair + kind
                                if m == 0:
                                    pe.wait_ge(panel[s], i * 16 + 16)
                                for k in range(KC):
                                    mm = pe.matmul(ps[:, bank, kind * S:(kind + 1) * S], panel_chan(s)[:, k, m * P:(m + 1) * P],
                                                   x_chan[:, k, :], start=(k == 0), stop=(k == KC - 1))
                                mm.then_inc(proj, 1)

            hidden(0, 2)
            pe.wait_ge(conv_steps, (W + 1) * PILOT)
            pe.wait_ge(pool_free, 2)
            pe.wait_ge(vec_taken, 2)
            for k in range(PILOT):
                mm = pe.matmul(ps[:, 7, 0:S], pilot_ones[:, :], conv[:, k, :], start=(k == 0), stop=(k == PILOT - 1))
            mm.then_inc(ch_stat, 1)
            hidden(2, 4)

            def residual_bias(tb, q):
                residual(tb, q)
                pe.matmul(ps[:, Q * tb + q, :], ones[0:1, :], bias_row[0:1, q * 512:(q + 1) * 512],
                          start=False, stop=True, skip_group_check=True)

            pe.wait_ge(glu_done, 4 + KC)
            pe.wait_ge(bias_loaded, 16)
            for b in range(6):
                residual_bias(b // Q, b % Q)
            pe.wait_ge(ch_steps, 1)
            for n, k in enumerate(CONV_ORDER):
                wait_shifted(pe, k)
                mm = pe.matmul(ps[:, 7, 0:S], mean_ones[:, :], conv[:, k, :], start=(n == 0), stop=(n == KC - 1), skip_group_check=True)
                if n == KC - 1:
                    mm.then_inc(ch_stat, 1)
                pe.wait_ge(squared, n + 1)
                mm = pe.matmul(ps[:, 6, 0:S], mean_ones[:, :], squares[:, k, :], start=(n == 0), stop=(n == KC - 1), skip_group_check=True)
            mm.then_inc(ch_stat, 1)
            pe.wait_ge(ch_steps, 2)
            residual_bias(1, 3)
            pe.wait_ge(ch_steps, 4)
            residual_bias(1, 2)
            split_tok(U_OUT, x_hi, conv_lo, lambda k: pe.wait_ge(conv_split, k + 1), True)

            def peer(layer):
                turn_x(1 + 2 * layer)
                pe.wait_ge(sk_loaded, 16 * (layer + 1))
                for j in range(HC // 4):
                    pe.wait_ge(x_split, 16 * layer + j + 1)
                    for c in range(4):
                        mm = pe.transpose(ps[:, j, c * P:(c + 1) * P], sk_raw[:, 4 * j + c, :], ident[:, :])
                    mm.then_inc(sk_ready, 1)
                pe.wait_ge(x_split, 16 * layer + 8)
                pe.wait_ge(sk_taken, 4 * (layer + 1))
                with pe.Fori(0, PANELS // RING) as i:
                    for s in range(RING):
                        for m in range(2):
                            j = 2 * s + m
                            pe.wait_ge(w_split, i * 8 + (U_WQ[layer] + j + 1))
                            pe.wait_ge(score_taken, i * 8 + (HC * layer + j + 1))
                            multiply_chan(U_WQ[layer] + j, j)
                        for m in range(2):
                            j = 2 * s + m
                            pe.wait_ge(chunk_taken, i * 8 + (8 + 48 * layer + j + 1))
                            for tb in range(TB):
                                mm = pe.matmul(ps[:, j, S + tb * P:S + (tb + 1) * P], q_now[:, j, tb * P:(tb + 1) * P],
                                               sk_t[:, bass.ds(i * 8 + j, 1), :].rearrange("p a b -> p (a b)"),
                                               start=True, stop=True)
                            mm.then_inc(score_ready, 1)
                pe.wait_ge(score_taken, 8 + HC * (layer + 1))
                for tb in range(TB):
                    for q in range(Q):
                        residual(tb, q)
                    base = (layer * TB + tb) * GROUPS
                    with pe.Fori(0, GROUPS) as i:
                        for s in range(RING):
                            pe.wait_ge(diag_done, i * RING + (base * RING + s + 1))
                            pe.wait_ge(v_row[s], i * 16 + (base + 1) * 16)
                            for q in range(Q):
                                mm = pe.matmul(ps[:, Q * tb + q, :], diag[:, s, :], row_tile(1, s)[:, q * 512:(q + 1) * 512],
                                               start=False, stop=True, skip_group_check=True)
                            mm.then_inc(v_used, 1)

            peer(0)

            turn_x(2)
            pe.wait_ge(x_split, 16)
            split_chan(U_K, 16)
            pe.wait_ge(chunk_taken, 8 + 32)
            split_tok(U_V, x_hi, x_lo, lambda k: None, False)
            pe.wait_ge(v_taken, 8)
            for t in range(-2, HEADS + 3):
                if t + 2 < HEADS:
                    h = t + 2
                    pe.wait_ge(w_split, U_Q + h + 1)
                    if h >= 2:
                        pe.wait_ge(chunk_taken, 8 + 32 + h - 1)
                    multiply_chan(U_Q + h, 6 + h % 2)
                if t == HEADS - 1:
                    pe.wait_ge(chunk_taken, 8 + 48)
                    for b in (6, 7):
                        residual(b // Q, b % Q)
                if 0 <= t + 1 < HEADS:
                    h = t + 1
                    pe.wait_ge(chunk_taken, 8 + 32 + h + 1)
                    if h >= 2:
                        pe.wait_ge(z_copied, h - 1)
                    pe.matmul(ps[:, h % 2, 0:S], k_t[:, h, 0:P], q_t[:, h, :], start=True, stop=True)
                    pe.matmul(ps[:, h % 2, S:AW], k_t[:, h, P:S], q_t[:, h, P:S], start=True, stop=True).then_inc(z_ready, 1)
                if 0 <= t - 3:
                    h = t - 3
                    b = 4 + h % 2
                    pe.wait_ge(att_masked, h + 1)
                    if h >= 2:
                        pe.wait_ge(o_split, h - 1)
                    pe.matmul(ps[:, b, 0:S], v_tok[:, 0, h * P:(h + 1) * P], att[:, h % 5, 0:S],
                              start=True, stop=False, skip_group_check=True)
                    pe.matmul(ps[:, b, P:S], v_tok[:, 1, h * P:(h + 1) * P], att[:, h % 5, S:AW],
                              start=False, stop=True, skip_group_check=True).then_inc(o_ready, 1)
                if 0 <= t - 1 < HEADS:
                    h = t - 1
                    b = 2 + h % 2
                    pe.wait_ge(z_soft, 2 * (h + 1))
                    if h >= 2:
                        pe.wait_ge(z_logit, h - 1)
                    pe.matmul(ps[:, b, 0:S], tri[:, :], soft[:, h % 3, 0:S], start=True, stop=False, skip_group_check=True)
                    pe.matmul(ps[:, b, P:S], ones[:, :], soft[:, h % 3, S:AW], start=False, stop=True, skip_group_check=True)
                    pe.matmul(ps[:, b, S:AW], tri[:, :], soft[:, h % 3, S:AW], start=True, stop=True,
                              skip_group_check=True).then_inc(rest_ready, 1)
            for b in range(6):
                if b == 4:
                    pe.wait_ge(o_split, HEADS)
                residual(b // Q, b % Q)
            split_tok(U_O, o_hi, o_lo, lambda k: None, True)
            peer(1)

        @block.scalar
        def _(act):
            act.sem_inc(chunk_taken, 8)
            act.sem_inc(score_taken, 8)

            def take_x(n):
                for b in range(8):
                    tb, j = b // Q, b % Q
                    act.wait_ge(xt_ready, 8 * n + b + 1)
                    to = x_hi if n else x_chan
                    act.activation(to[:, 4 * j:4 * j + 4, tb * P:(tb + 1) * P],
                                   ps[:, b, :].rearrange("p (a b) -> p a b", a=4), ACT.Copy).then_inc(xt_taken, 1)

            def norm(n, tb):
                if tb == 0 or n % 2:
                    act.preload_act_table(ACT.Sqrt)
                v = lnv[:, tb, :]
                act.wait_ge(ln_steps[n], LN_STEPS * tb + 6)
                act.activation(v[:, 1:2], v[:, 0:1], ACT.Sqrt).then_inc(ln_act[n], 1)

            def round_half(u):
                if u % 2 == 0:
                    n = P_OUT + u // 2
                    act.wait_ge(panel[n % 2], 16 * landed(n))
                act.wait_ge(proj, buffer_free(u))
                act.activation(half_as(w_hi, u), raw_half(u), ACT.Copy).then_inc(w_rounded, 1)

            def gate_exp(layer, tb, half):
                act.wait_ge(route[layer], part_at(tb, half) + PART_LOGITS)
                part = logits[:, half * (PH // 2):(half + 1) * (PH // 2), :]
                act.activation(part, part, ACT.Exp).then_inc(route_exp, 1)

            take_x(0)
            act.wait_ge(vec_t, 1)
            act.activation(vec[:, :], ps[:, 6, 0:NB_IN + 3 * KC], ACT.Copy).then_inc(vec_taken, 1)
            act.wait_ge(vec_t, 2)
            act.activation(taps[:, :], ps[:, 7, 0:W * KC], ACT.Copy).then_inc(vec_taken, 1)
            act.wait_ge(vec_taken, 2)

            with act.Fori(0, KC // 4) as i:
                for b in range(4):
                    act.wait_ge(proj, i * 8 + (2 * b + 2))
                    act.sem_inc(act_tick, 1)
                    act.wait_ge(glu_done, i * 4 + (b + 3))
                    act.sem_inc(act_tick, 1)
                    act.activation(sig[:, b % 2, :], ps[:, b, S:2 * S], ACT.Sigmoid,
                                   bias=vec[:, bass.ds(i * 4 + (KC + b), 1)]).then_inc(sig_ready, 1)

            for q in range(2):
                act.wait_ge(shifted, 4 * q + 4)
                act.activation(squares[:, 4 * q:4 * q + 4, :], conv[:, 4 * q:4 * q + 4, :], ACT.Square).then_inc(squared, 4)
            for k in CONV_ORDER[KC // 2:]:
                if k == CONV_ORDER[-1]:
                    for u in range(2):
                        round_half(U_OUT + u)
                wait_shifted(act, k)
                act.activation(squares[:, k, :], conv[:, k, :], ACT.Square).then_inc(squared, 1)
            act.preload_act_table(ACT.Sqrt)
            act.wait_ge(ch_steps, 4)
            act.activation(ch_rstd[:, 1, :], ch_rstd[:, 0, :], ACT.Sqrt).then_inc(ch_act, 1)
            act.preload_act_table(ACT.Silu)

            def swish(k):
                act.wait_ge(ch_steps, CH_DIVIDED[k // 4])
                act.activation(conv[:, k, :], conv[:, k, :], ACT.Silu, scale=vec[:, NB_IN + KC + k:NB_IN + KC + k + 1],
                               bias=vec[:, NB_IN + 2 * KC + k:NB_IN + 2 * KC + k + 1]).then_inc(ch_act, 1)
                act.wait_ge(ch_act, 2 * k + 2)
                act.activation(x_hi[:, k, :], conv[:, k, :], ACT.Copy).then_inc(ch_act, 1)

            for k in range(4):
                swish(k)
            for u in range(2, HALVES):
                round_half(U_OUT + u)
                if u + 2 < KC:
                    swish(u + 2)

            def peer(layer):
                norm(2 * layer, 0)
                for u in range(2):
                    round_half(U_WQ[layer] + u)
                norm(2 * layer, 1)
                take_x(1 + 2 * layer)
                for j in range(4):
                    act.wait_ge(sk_ready, 4 * layer + j + 1)
                    act.activation(sk_t[:, 4 * j:4 * j + 4, :], ps[:, j, :].rearrange("p (a b) -> p a b", a=4),
                                   ACT.Copy).then_inc(sk_taken, 1)
                for c in range(0, HC, 2):
                    for m in range(c, c + 2):
                        act.wait_ge(proj, 2 * P_WQ[layer] + m + 1)
                        if m >= 8:
                            act.wait_ge(score_ready, HC * layer + m - 7)
                        act.activation(q_now[:, m % 8, :], ps[:, m % 8, 0:S], ACT.Copy).then_inc(chunk_taken, 1)
                        if m + 2 < HALVES:
                            round_half(U_WQ[layer] + m + 2)
                    for m in range(c, c + 2):
                        act.wait_ge(score_ready, HC * layer + m + 1)
                        act.activation(score[:, :, m * NKEY:(m + 1) * NKEY],
                                       ps[:, m % 8, S:2 * S].rearrange("p (t k) -> p t k", t=TB), ACT.Copy).then_inc(score_taken, 1)
                    if c == 2 * EARLY_HEADS:
                        gate_exp(layer, 0, 0)

                def coefficients(tb, half, first, last):
                    base = (layer * TB + tb) * GROUPS + half * (GROUPS // 2)
                    with act.Fori(first, last) as i:
                        act.wait_ge(u_used, i * RING + (base * RING + 2 * RING))
                        act.activation(gelu_now[:, :], h_now[:, :], ACT.Gelu).then_inc(gelu_done, 1)
                        act.wait_ge(coef_done, i + (base + 1))
                        for s in range(RING):
                            act.wait_ge(v_used, i * RING + (base * RING + s + 1))
                            act.activation(diag[:, s, :], ident[:, :], ACT.Copy, scale=coef_now[:, s:s + 1]).then_inc(diag_done, 1)

                coefficients(0, 0, 0, 1)
                gate_exp(layer, 0, 1)
                for tb in range(TB):
                    for half in range(2):
                        coefficients(tb, half, 0 if half else 1, GROUPS // 2)
                        if tb == 0:
                            gate_exp(layer, 1, half)
                    if tb == 0:
                        coefficients(1, 0, 0, 1)
                    norm(2 * layer + 1, tb)

            peer(0)
            for u in range(2):
                round_half(U_K + u)
            take_x(2)
            for u in range(U_K + 2, U_Q + 2):
                round_half(u)
                c = u - 2
                if c < U_V:
                    act.wait_ge(proj, IN_HALVES + c + 1)
                    act.activation(k_t[:, c - U_K, :], ps[:, c % 8, 0:S], ACT.Copy).then_inc(chunk_taken, 1)
                elif c == U_Q - 1:
                    act.wait_ge(first_sum, 2)
                    for b in range(8):
                        if b == Q:
                            act.wait_ge(proj, 2 * P_Q)
                        act.activation(v_tok[:, b // Q, (b % Q) * 512:(b % Q + 1) * 512], ps[:, b, :], ACT.Copy).then_inc(v_taken, 1)
            act.preload_act_table_set("natural_log_exp_and_others")
            for t in range(-1, HEADS + 3):
                if t + 3 < HEADS + 2:
                    round_half(U_Q + t + 3)
                if t + 1 < HEADS:
                    h = t + 1
                    act.wait_ge(proj, IN_HALVES + U_Q + h + 1)
                    act.activation(q_t[:, h, :], ps[:, 6 + h % 2, 0:S], ACT.Copy, scale=SCALE).then_inc(chunk_taken, 1)
                if 0 <= t - 2 < HEADS:
                    h = t - 2
                    act.wait_ge(z_logit, h + 1)
                    act.activation(att[:, h % 5, :], att[:, h % 5, :], ACT.Exp).then_inc(att_exp, 1)
                if 0 <= t - 3:
                    h = t - 3
                    act.wait_ge(o_ready, h + 1)
                    act.activation(o_hi[:, h, :], ps[:, 4 + h % 2, 0:S], ACT.Copy).then_inc(o_copied, 1)
                if 0 <= t < HEADS:
                    h = t
                    act.wait_ge(z_abs, h + 1)
                    act.activation(soft[:, h % 3, :], soft[:, h % 3, :], ACT.Exp, scale=-1.0).then_inc(z_log, 1)
                    act.wait_ge(z_log, 2 * h + 1)
                    act.activation(soft[:, h % 3, :], soft[:, h % 3, :], ACT.Ln, bias=1.0).then_inc(z_log, 1)
                if t + 1 < HEADS:
                    h = t + 1
                    act.wait_ge(z_ready, h + 1)
                    if h >= 5:
                        act.wait_ge(o_ready, h - 4)
                    act.activation(att[:, h % 5, :], ps[:, h % 2, 0:AW], ACT.Copy).then_inc(z_copied, 1)
            for u in range(2, HALVES):
                round_half(U_O + u)
            peer(1)

        @block.vector
        def _(dve):
            dve.sem_inc(u_used, RING)
            dve.sem_inc(glu_done, 4)

            dve.memset(hpad[:, :, 0:PAD], 0.0).then_inc(conv_steps, W + 1)
            dve.wait_ge(vec_taken, 2)
            taps_by = taps[:, :].rearrange("p (w c) -> p w c", c=KC)
            STEPS = W + 1
            def convolve(first, last):
                with dve.Fori(first, last) as i:
                    def gated(b, to):
                        dve.wait_ge(sig_ready, i * 4 + (b + 1))
                        dve.scalar_tensor_tensor(out=to, in0=ps[:, b, 0:S], scalar=vec[:, bass.ds(i * 4 + b, 1)],
                                                 in1=sig[:, b % 2, :], op0=ALU.add, op1=ALU.mult).then_inc(glu_done, 1)

                    dve.wait_ge(pool_free, i + 1)
                    gated(0, pool_pad[:, PAD:])
                    dve.tensor_copy(pool_tap[:, 0:W], taps_by[:, :, bass.ds(i * 4, 1)].rearrange("p w c -> p (w c)")) \
                       .then_inc(pool_fed, 1)
                    dve.tensor_copy(pool_tap[:, W:], vec[:, bass.ds(i * 4 + NB_IN, 1)]).then_inc(pool_fed, 1)
                    for b in range(1, 4):
                        e = b % 2
                        at = b * STEPS
                        dve.wait_ge(conv_steps, i * (3 * STEPS) + at)
                        gated(b, hpad[:, e, PAD:])
                        dve.tensor_copy(tap_c[:, e, :], taps_by[:, :, bass.ds(i * 4 + b, 1)].rearrange("p w c -> p (w c)")) \
                           .then_inc(conv_steps, 1)
                        dve.wait_ge(conv_steps, i * (3 * STEPS) + (at + 1))
                        dve.wait_ge(glu_done, i * 4 + (4 + b + 1))
                        dve.tensor_scalar(acc_c[:, e, :], hpad[:, e, 0:S], tap_c[:, e, 0:1],
                                          vec[:, bass.ds(i * 4 + (NB_IN + b), 1)], ALU.mult, ALU.add).then_inc(conv_steps, 1)
                        for w in range(1, W):
                            dve.wait_ge(conv_steps, i * (3 * STEPS) + (at + 1 + w))
                            to = acc_c[:, e, :] if w < W - 1 else conv[:, bass.ds(i * 4 + b, 1), :].rearrange("p a b -> p (a b)")
                            dve.scalar_tensor_tensor(out=to, in0=hpad[:, e, w:w + S], scalar=tap_c[:, e, w:w + 1],
                                                     in1=acc_c[:, e, :], op0=ALU.mult, op1=ALU.add).then_inc(conv_steps, 1)
                        if first:
                            dve.wait_ge(conv_steps, i * (3 * STEPS) + (at + STEPS))
                            chunk = conv[:, bass.ds(i * 4 + b, 1), :].rearrange("p a b -> p (a b)")
                            dve.tensor_tensor(out=chunk, in0=chunk, in1=pilot, op=ALU.subtract).then_inc(shifted, 1)

            convolve(0, 2)
            dve.wait_ge(ch_stat, 1)
            dve.tensor_copy(pilot, ps[:, 7, 0:S]).then_inc(ch_steps, 1)
            dve.wait_ge(ch_steps, 1)
            dve.wait_ge(conv_steps, STEPS * (6 + 1))
            dve.wait_ge(pool_free, 3)
            for q in range(2):
                c = conv[:, 4 * q:4 * q + 4, :]
                dve.tensor_tensor(out=c, in0=c, in1=pilot.unsqueeze(1).to_broadcast([P, 4, S]), op=ALU.subtract).then_inc(shifted, 4)
            convolve(2, 4)

            dve.wait_ge(ch_stat, 2)
            dve.tensor_copy(ch_mean, ps[:, 7, 0:S]).then_inc(ch_steps, 1)
            dve.wait_ge(ch_steps, 2)
            dve.tensor_tensor(out=ch_msq, in0=ch_mean, in1=ch_mean, op=ALU.mult).then_inc(ch_steps, 1)
            dve.wait_ge(ch_steps, 3)
            dve.wait_ge(ch_stat, 3)
            dve.scalar_tensor_tensor(out=ch_rstd[:, 0, :], in0=ps[:, 6, 0:S], scalar=LN_EPS, in1=ch_msq,
                                     op0=ALU.add, op1=ALU.subtract).then_inc(ch_steps, 1)

            def centre(q):
                c = conv[:, 4 * q:4 * q + 4, :]
                dve.tensor_tensor(out=c, in0=c, in1=ch_mean.unsqueeze(1).to_broadcast([P, 4, S]), op=ALU.subtract).then_inc(ch_steps, 1)

            def divide(q):
                dve.wait_ge(ch_steps, CH_DIVIDED[q] - 1)
                c = conv[:, 4 * q:4 * q + 4, :]
                dve.tensor_tensor(out=c, in0=c, in1=ch_rstd[:, 0:1, :].to_broadcast([P, 4, S]), op=ALU.mult).then_inc(ch_steps, 1)

            dve.wait_ge(shifted, KC - 2)
            dve.wait_ge(squared, KC)
            centre(0)
            dve.wait_ge(ch_act, 1)
            dve.reciprocal(ch_rstd[:, 0, :], ch_rstd[:, 1, :]).then_inc(ch_steps, 1)
            divide(0)

            def conv_low(k):
                dve.wait_ge(ch_act, 2 * k + 3)
                dve.tensor_tensor(out=conv_lo[:, k, :], in0=conv[:, k, :], in1=x_hi[:, k, :].bitcast(F32),
                                  op=ALU.subtract).then_inc(conv_split, 1)

            def split_half(u):
                dve.wait_ge(w_rounded, u + 1)
                dve.wait_ge(proj, buffer_free(u))
                dve.tensor_tensor(out=half_as(w_lo, u), in0=raw_half(u), in1=half_as(w_hi, u).bitcast(F32),
                                  op=ALU.subtract).then_inc(w_split, 1)

            centre(1)
            conv_low(0)
            divide(1)
            for k in range(1, 4):
                conv_low(k)
            for q in range(2, 4):
                centre(q)
                divide(q)
            dve.wait_ge(w_split, U_OUT + 2)
            for u in range(2, HALVES):
                split_half(U_OUT + u)
                if u + 2 < KC:
                    conv_low(u + 2)

            def norm(n, tb, wait_bank):
                at = LN_STEPS * tb
                for q in range(Q):
                    wait_bank(q)
                    dve.bn_stats(stats[:, tb, q, :], ps[:, Q * tb + q, :]).then_inc(ln_steps[n], 1)
                dve.wait_ge(ln_steps[n], at + 4)
                dve.bn_aggr(mv[:, tb, :], stats[:, tb, :, :]).then_inc(ln_steps[n], 1)
                dve.wait_ge(ln_steps[n], at + 5)
                dve.tensor_scalar(lnv[:, tb, 0:1], mv[:, tb, 1:2], LN_EPS, None, ALU.add).then_inc(ln_steps[n], 1)
                dve.wait_ge(rows_loaded, 32 * (n + 1))
                dve.scalar_tensor_tensor(out=x_tok[:, tb, :], in0=bank_cols(tb), scalar=mv[:, tb, 0:1], in1=ln_rows[:, 0, :],
                                         op0=ALU.subtract, op1=ALU.mult).then_inc(ln_steps[n], 1)
                dve.wait_ge(ln_act[n], tb + 1)
                dve.reciprocal(lnv[:, tb, 2:3], lnv[:, tb, 1:2]).then_inc(ln_steps[n], 1)
                dve.wait_ge(ln_steps[n], at + LN_HEAD)
                for q in range(Q):
                    cols = slice(q * 512, (q + 1) * 512)
                    dve.scalar_tensor_tensor(out=x_tok[:, tb, cols], in0=x_tok[:, tb, cols], scalar=lnv[:, tb, 2:3],
                                             in1=ln_rows[:, 1, cols], op0=ALU.mult, op1=ALU.add).then_inc(ln_steps[n], 1)

            def top16(values, indices, table, rows, at, done):
                for r in range(rows):
                    dve.max(values(r)[:, 0:8], table(r)).then_inc(done, 1)
                dve.wait_ge(done, at + rows)
                for r in range(rows):
                    dve.max_index(indices(r)[:, 0:8], values(r)[:, 0:8], table(r)).then_inc(done, 1)
                dve.wait_ge(done, at + 2 * rows)
                for r in range(rows):
                    dve.match_replace(table(r), values(r)[:, 0:8], table(r), -3.0e38).then_inc(done, 1)
                dve.wait_ge(done, at + 3 * rows)
                for r in range(rows):
                    dve.max(values(r)[:, 8:16], table(r)).then_inc(done, 1)
                dve.wait_ge(done, at + 4 * rows)
                for r in range(rows):
                    dve.max_index(indices(r)[:, 8:16], values(r)[:, 8:16], table(r)).then_inc(done, 1)
                dve.wait_ge(done, at + 5 * rows)

            def route_head(layer, h):
                done = route[layer]
                at = head_at(h)
                dve.wait_ge(score_taken, 8 + HC * layer + 2 * h + 2)
                top16(lambda r: key_s[:, r // 2, 2 * h + r % 2, :], lambda r: key_i[:, r // 2, 2 * h + r % 2, :],
                      lambda r: score[:, r // 2, (2 * h + r % 2) * NKEY:(2 * h + r % 2 + 1) * NKEY], 2 * TB, at, done)
                dve.tensor_tensor(out=pair_s[:, :, :].rearrange("p t (a b) -> p t a b", a=TOPK),
                                  in0=key_s[:, :, 2 * h, :].unsqueeze(3).to_broadcast([P, TB, TOPK, TOPK]),
                                  in1=key_s[:, :, 2 * h + 1, :].unsqueeze(2).to_broadcast([P, TB, TOPK, TOPK]),
                                  op=ALU.add).then_inc(done, 1)
                dve.wait_ge(done, at + 21)
                top16(lambda r: best_s[:, r, h, :], lambda r: best_j[:, r, h, :], lambda r: pair_s[:, r, :], TB, at + 21, done)

            def route_part(layer, tb, half):
                done = route[layer]
                at = part_at(tb, half)
                HH, HS = PH // 2, SLOTS // 2
                heads, slots = slice(half * HH, (half + 1) * HH), slice(half * HS, (half + 1) * HS)
                best = best_s[:, tb, heads, :]
                dve.tensor_tensor(out=logits[:, heads, :], in0=best, in1=best[:, :, 0:1].to_broadcast([P, HH, TOPK]),
                                  op=ALU.subtract).then_inc(done, 1)
                flat_j = best_j[:, tb, heads, :].rearrange("p h k -> p (h k)")
                dve.tensor_scalar(row_j[:, 0, slots], flat_j, 4, None, ALU.logical_shift_right).then_inc(done, 1)
                dve.tensor_scalar(row_j[:, 1, slots], flat_j, TOPK - 1, None, ALU.bitwise_and).then_inc(done, 1)
                dve.wait_ge(done, at + 3)
                dve.tensor_copy(row_f[:, 0, slots], row_j[:, 0, slots]).then_inc(done, 1)
                dve.tensor_copy(row_f[:, 1, slots], row_j[:, 1, slots]).then_inc(done, 1)
                key_rows = slice(half * (HC // 2), (half + 1) * (HC // 2))
                dve.tensor_copy(key_f[:, key_rows, :], key_i[:, tb, key_rows, :]).then_inc(done, 1)
                dve.wait_ge(done, at + 6)
                keys = key_f[:, key_rows, :].rearrange("p (h c) k -> p h c k", c=2)
                hot_s = hot[:, slots, :]
                hot_hk = hot_s.rearrange("p (h k) a -> p h k a", h=HH)
                for c in range(2):
                    dve.tensor_tensor(out=hot_s, in0=row_f[:, c, slots].unsqueeze(2).to_broadcast([P, HS, TOPK]),
                                      in1=iota_f[:, :].unsqueeze(1).to_broadcast([P, HS, TOPK]), op=ALU.is_equal).then_inc(done, 1)
                    dve.wait_ge(done, at + 7 + 3 * c)
                    dve.tensor_tensor(out=hot_hk, in0=hot_hk, in1=keys[:, :, c, :].unsqueeze(2).to_broadcast([P, HH, TOPK, TOPK]),
                                      op=ALU.mult).then_inc(done, 1)
                    dve.wait_ge(done, at + 8 + 3 * c)
                    dve.tensor_reduce(row_e[:, c, slots], hot_s, AX_X, ALU.add).then_inc(done, 1)
                    dve.wait_ge(done, at + 9 + 3 * c)
                dve.scalar_tensor_tensor(out=row_e[:, 0, slots], in0=row_e[:, 0, slots], scalar=float(NKEY), in1=row_e[:, 1, slots],
                                         op0=ALU.mult, op1=ALU.add).then_inc(done, 1)
                dve.wait_ge(done, at + 13)
                dve.tensor_scalar(index[:, tb, slots], row_e[:, 0, slots], float(layer * NEXP), None, ALU.add).then_inc(done, 1)
                dve.wait_ge(route_exp, 2 * TB * layer + 2 * tb + half + 1)
                dve.tensor_reduce(gsum[:, 0, heads], logits[:, heads, :], AX_X, ALU.add).then_inc(done, 1)
                dve.wait_ge(done, at + 15)
                dve.reciprocal(gsum[:, 1, heads], gsum[:, 0, heads]).then_inc(done, 1)
                dve.wait_ge(done, at + 16)
                dve.tensor_tensor(out=gate[:, tb, slots].rearrange("p (h k) -> p h k", k=TOPK), in0=logits[:, heads, :],
                                  in1=gsum[:, 1, heads].unsqueeze(2).to_broadcast([P, HH, TOPK]), op=ALU.mult).then_inc(done, 1)
                dve.wait_ge(done, at + 17)

            def x_low(n):
                for b in range(8):
                    tb, j = b // Q, b % Q
                    dve.wait_ge(xt_taken, 8 * n + b + 1)
                    part = (slice(None), slice(4 * j, 4 * j + 4), slice(tb * P, (tb + 1) * P))
                    dve.tensor_tensor(out=x_lo[part], in0=ps[:, b, :].rearrange("p (a b) -> p a b", a=4),
                                      in1=x_hi[part].bitcast(F32), op=ALU.subtract).then_inc(x_split, 1)

            def peer(layer):
                def sublayer_sum(tb, q):
                    if q < Q - 1:
                        dve.wait_ge(bank_sum, ((Q - 1) * TB) * 2 * layer + (Q - 1) * tb + q + 1)
                    elif tb == 0:
                        dve.wait_ge(first_sum, 2 * layer + 1)
                    else:
                        dve.wait_ge(proj, 2 * P_WQ[layer])

                def mixer_sum(tb, q):
                    if q == 0:
                        dve.wait_ge(v_used, RING + (layer * TB + tb + 1) * SLOTS)

                for tb in range(TB):
                    norm(2 * layer, tb, lambda q: sublayer_sum(tb, q))
                x_low(1 + 2 * layer)

                def dots(tb, half, first, last):
                    base = (layer * TB + tb) * GROUPS + half * (GROUPS // 2)
                    with dve.Fori(first, last) as i:
                        for s in range(RING):
                            dve.wait_ge(u_row[s], i * 16 + (base + 1) * 16)
                            dve.scalar_tensor_tensor(out=row_tile(0, s), in0=row_tile(0, s), scalar=1.0, in1=x_tok[:, tb, :],
                                                     op0=ALU.mult, op1=ALU.mult, accum_out=h_now[:, s:s + 1]).then_inc(u_used, 1)
                        if layer or tb or half or first:
                            dve.wait_ge(diag_done, i * RING + base * RING)
                        dve.wait_ge(gelu_done, i + (base + 1))
                        dve.tensor_tensor(out=coef_now[:, :], in0=gelu_now[:, :],
                                          in1=gate[:, tb, bass.ds(i * RING + half * (SLOTS // 2), RING)],
                                          op=ALU.mult).then_inc(coef_done, 1)

                for h in range(PH):
                    if h == EARLY_HEADS:
                        route_part(layer, 0, 0)
                    if h == PH - 1:
                        dots(0, 0, 0, 1)
                    route_head(layer, h)
                route_part(layer, 0, 1)
                for tb in range(TB):
                    for half in range(2):
                        dots(tb, half, 0 if half else 1, GROUPS // 2)
                        if tb == 0:
                            route_part(layer, 1, half)
                    if tb == 0:
                        dots(1, 0, 0, 1)
                    norm(2 * layer + 1, tb, lambda q: mixer_sum(tb, q))

            peer(0)

            dve.wait_ge(w_split, U_K)
            split_half(U_K)
            x_low(2)
            for u in range(U_K + 1, U_Q + 2):
                split_half(u)

            for t in range(-1, HEADS + 3):
                if t + 3 < HEADS + 2:
                    split_half(U_Q + t + 3)
                if 0 <= t - 2 < HEADS:
                    h = t - 2
                    dve.wait_ge(rest_ready, h + 1)
                    dve.tensor_tensor(out=att[:, h % 5, :], in0=att[:, h % 5, :], in1=ps[:, 2 + h % 2, 0:AW],
                                      op=ALU.subtract).then_inc(z_logit, 1)
                if 0 <= t < HEADS:
                    h = t
                    z = att[:, h % 5, :]
                    dve.wait_ge(z_copied, h + 1)
                    if h >= 3:
                        dve.wait_ge(rest_ready, h - 2)
                    dve.scalar_tensor_tensor(out=soft[:, h % 3, :], in0=z, scalar=-1.0, in1=z,
                                             op0=ALU.mult, op1=ALU.max).then_inc(z_abs, 1)
                if 0 <= t - 1 < HEADS:
                    h = t - 1
                    s = soft[:, h % 3, :]
                    dve.wait_ge(z_log, 2 * h + 2)
                    dve.scalar_tensor_tensor(out=s, in0=att[:, h % 5, :], scalar=0.0, in1=s,
                                             op0=ALU.max, op1=ALU.add).then_inc(z_soft, 1)
                    dve.wait_ge(z_soft, 2 * h + 1)
                    diagonal = s.rearrange("p (a b) -> p a b", b=P)[:, 0:3:2, :]
                    dve.tensor_tensor(out=diagonal, in0=diagonal, in1=causal[:, :].unsqueeze(1).to_broadcast([P, 2, P]),
                                      op=ALU.mult).then_inc(z_soft, 1)
                if 0 <= t - 2 < HEADS:
                    h = t - 2
                    dve.wait_ge(att_exp, h + 1)
                    diagonal = att[:, h % 5, :].rearrange("p (a b) -> p a b", b=P)[:, 0:3:2, :]
                    dve.scalar_tensor_tensor(out=diagonal, in0=diagonal, scalar=1.0,
                                             in1=causal[:, :].unsqueeze(1).to_broadcast([P, 2, P]),
                                             op0=ALU.min, op1=ALU.mult).then_inc(att_masked, 1)
                if 0 <= t - 3:
                    h = t - 3
                    dve.wait_ge(o_copied, h + 1)
                    dve.tensor_tensor(out=o_lo[:, h, :], in0=ps[:, 4 + h % 2, 0:S], in1=o_hi[:, h, :].bitcast(F32),
                                      op=ALU.subtract).then_inc(o_split, 1)
            for u in range(2, HALVES):
                split_half(U_O + u)
            peer(1)


_INS = ["x", "conv_w_in", "conv_b_in", "conv_w_dw", "conv_b_dw", "conv_ln_g", "conv_ln_b", "conv_w_out", "conv_b_out",
        "attn_w_kv", "attn_w_q", "attn_w_o", "peer_w_q", "peer_sub_keys", "peer_u", "peer_v", "ln_g", "ln_b"]


def kernel(**inputs):
    import numpy as np
    import concourse.bacc as bacc
    from concourse.bass_utils import run_bass_kernel_spmd

    nc = bacc.Bacc("TRN2", target_bir_lowering=False, num_devices=1)
    arrays, args = {}, []
    for name in _INS:
        a = np.ascontiguousarray(inputs[name])
        arrays[f"in_{name}"] = a
        args.append(nc.dram_tensor(f"in_{name}", a.shape, mybir.dt.from_np(a.dtype), kind="ExternalInput").ap())
    out = nc.dram_tensor("out_dram", inputs["x"].shape, F32, kind="ExternalOutput").ap()
    build(nc, *args, out)
    r = run_bass_kernel_spmd(nc, [arrays], core_ids=[0])
    return r.results[0]["out_dram"]
```
